# Optimizing a Trainium2 kernel written in Bass

```python
import math
import jax, jax.numpy as jnp
from jax import lax
import numpy as np

D_MODEL = 1024
BATCH = 1
SEQ = 1024
DEPTH = 1
DEC_BATCH = 8
DEC_SEQ = 1
PAST_LEN = 4096
PAGE_SIZE = 128

D_CONV = 512
CONV_W = 3
N_HEADS = 8
Q_LORA = 384
KV_LORA = 256
NOPE_DIM = 64
ROPE_DIM = 32
V_DIM = 64
QK_DIM = NOPE_DIM + ROPE_DIM
ROPE_BASE = 10000.0
ATTN_SCALE = QK_DIM ** -0.5
Q_BLOCK = 128
N_GROUPS = 4
EXP_PER_GROUP = 8
N_EXPERTS = N_GROUPS * EXP_PER_GROUP
TOP_K = 2
D_EXPERT = 512
MOE_BLOCK = 128
DN_ALPHA = (2 * DEPTH) ** 0.25
DN_BETA = (8 * DEPTH) ** -0.25
LN_EPS = 1e-5
RMS_EPS = 1e-6
_IN_SPLITS = (D_CONV, 2 * D_CONV, 3 * D_CONV, 3 * D_CONV + Q_LORA,
              3 * D_CONV + Q_LORA + KV_LORA, 3 * D_CONV + Q_LORA + KV_LORA + ROPE_DIM,
              3 * D_CONV + Q_LORA + KV_LORA + ROPE_DIM + D_MODEL)
IN_COLS = 3 * D_CONV + Q_LORA + KV_LORA + ROPE_DIM + 2 * D_MODEL

kernel_name = 'hybrid_conv_mla_hmoe_step'

def _layernorm(x, g, b):
    xf = x.astype(jnp.float32)
    mu = jnp.mean(xf, axis=-1, keepdims=True)
    var = jnp.mean(jnp.square(xf - mu), axis=-1, keepdims=True)
    return ((xf - mu) * lax.rsqrt(var + LN_EPS) * g.astype(jnp.float32) + b.astype(jnp.float32)).astype(x.dtype)

def _rmsnorm(x, g):
    xf = x.astype(jnp.float32)
    return (xf * lax.rsqrt(jnp.mean(xf * xf, axis=-1, keepdims=True) + RMS_EPS) * g.astype(jnp.float32)).astype(x.dtype)

def _rope_tables(pos):
    half = ROPE_DIM // 2
    inv = ROPE_BASE ** (-(jnp.arange(half, dtype=jnp.float32) * 2.0 / ROPE_DIM))
    ang = pos.astype(jnp.float32)[:, None] * inv[None, :]
    return jnp.cos(ang), jnp.sin(ang)

def _rope(x, cos, sin):
    x1, x2 = jnp.split(x.astype(jnp.float32), 2, axis=-1)
    return jnp.concatenate([x1 * cos - x2 * sin, x1 * sin + x2 * cos], axis=-1).astype(x.dtype)

def _in_proj(x, pos, w_in, q_norm_g, w_uq, kv_norm_g):
    n, t, _ = x.shape
    p = x @ w_in
    b_g, c_g, h, cq, ckv, kr, g_conv, g_attn = jnp.split(p, _IN_SPLITS, axis=-1)
    q = (_rmsnorm(cq, q_norm_g) @ w_uq).reshape(n, t, N_HEADS, QK_DIM)
    cos, sin = _rope_tables(pos)
    q_nope = q[..., :NOPE_DIM]
    q_rope = _rope(q[..., NOPE_DIM:], cos[:, None, :], sin[:, None, :])
    ckv = _rmsnorm(ckv, kv_norm_g)
    kr = _rope(kr, cos, sin)
    return b_g, c_g * h, q_nope, q_rope, ckv, kr, g_conv, g_attn

def _prompt_attention(q_nope, q_rope, ckv, kr, w_uk, w_uv):
    n, t = q_nope.shape[:2]
    k_nope = jnp.einsum('btc,chd->bthd', ckv, w_uk)
    v = jnp.einsum('btc,chd->bthd', ckv, w_uv)
    nb = t // Q_BLOCK

    def blocks(a):
        return jnp.moveaxis(a.reshape((n, nb, Q_BLOCK) + a.shape[2:]), 1, 0)

    kpos = jnp.arange(t)

    def one(args):
        qn, qr, i = args
        s = (jnp.einsum('bqhd,bkhd->bhqk', qn, k_nope)
             + jnp.einsum('bqhr,bkr->bhqk', qr, kr)).astype(jnp.float32) * ATTN_SCALE
        qpos = i * Q_BLOCK + jnp.arange(Q_BLOCK)
        s = jnp.where(kpos[None, :] <= qpos[:, None], s, -jnp.inf)
        pr = jax.nn.softmax(s, axis=-1).astype(v.dtype)
        return jnp.einsum('bhqk,bkhd->bqhd', pr, v)

    o = lax.map(one, (blocks(q_nope), blocks(q_rope), jnp.arange(nb)))
    return jnp.moveaxis(o, 0, 1).reshape(n, t, N_HEADS, V_DIM)

def _sample_attention(q_nope, q_rope, ckv_new, kr_new, past_c, past_r, w_uk, w_uv):
    ts = q_nope.shape[1]
    past = past_c.shape[1]
    keys_c = jnp.concatenate([past_c.astype(ckv_new.dtype), ckv_new], axis=1)
    keys_r = jnp.concatenate([past_r.astype(kr_new.dtype), kr_new], axis=1)
    q_lat = jnp.einsum('bthd,chd->bthc', q_nope, w_uk)
    s = (jnp.einsum('bthc,blc->bhtl', q_lat, keys_c)
         + jnp.einsum('bthr,blr->bhtl', q_rope, keys_r)).astype(jnp.float32) * ATTN_SCALE
    kpos = jnp.arange(past + ts)
    qpos = past + jnp.arange(ts)
    s = jnp.where(kpos[None, :] <= qpos[:, None], s, -jnp.inf)
    pr = jax.nn.softmax(s, axis=-1).astype(keys_c.dtype)
    o_lat = jnp.einsum('bhtl,blc->bthc', pr, keys_c)
    return jnp.einsum('bthc,chd->bthd', o_lat, w_uv)

def _merge(b_g, u_ext, o, g_conv, g_attn, conv_w, w_br_conv, w_br_attn, w_o):
    n, t = o.shape[:2]
    conv = conv_w[0] * u_ext[:, 0:t]
    for k in range(1, CONV_W):
        conv = conv + conv_w[k] * u_ext[:, k:k + t]
    y_conv = (b_g * conv) @ w_br_conv
    y_attn = o.reshape(n, t, N_HEADS * V_DIM) @ w_br_attn
    m = jax.nn.sigmoid(g_conv) * y_conv + jax.nn.sigmoid(g_attn) * y_attn
    return m @ w_o

def _moe(x, router_w_group, router_b_group, router_w_expert, router_b_expert, w_gate, w_up, w_down):
    shp = x.shape
    xt = x.reshape(-1, D_MODEL)
    t = xt.shape[0]
    lg = (xt @ router_w_group).astype(jnp.float32) + router_b_group.astype(jnp.float32)
    pg = jax.nn.softmax(lg, axis=-1)
    grp = jnp.argmax(pg, axis=-1)
    p_grp = jnp.max(pg, axis=-1)
    le = ((xt @ router_w_expert).astype(jnp.float32) + router_b_expert.astype(jnp.float32)).reshape(t, N_GROUPS, EXP_PER_GROUP)
    le = jnp.take_along_axis(le, grp[:, None, None], axis=1)[:, 0]
    top_l, top_i = lax.top_k(le, TOP_K)
    wts = p_grp[:, None] * jax.nn.softmax(top_l, axis=-1)
    eid = grp[:, None] * EXP_PER_GROUP + top_i
    a = t * TOP_K
    eid_f = eid.reshape(a)
    tok_f = jnp.repeat(jnp.arange(t, dtype=jnp.int32), TOP_K)
    wt_f = wts.reshape(a)
    order = jnp.argsort(eid_f)
    e_s, t_s, w_s = eid_f[order], tok_f[order], wt_f[order]
    counts = jnp.zeros((N_EXPERTS,), jnp.int32).at[eid_f].add(1)
    start = jnp.cumsum(counts) - counts
    pcounts = (counts + MOE_BLOCK - 1) // MOE_BLOCK * MOE_BLOCK
    pend = jnp.cumsum(pcounts)
    pstart = pend - pcounts
    dest = pstart[e_s] + jnp.arange(a, dtype=jnp.int32) - start[e_s]
    n_blocks = -(-a // MOE_BLOCK) + N_EXPERTS
    n_slots = n_blocks * MOE_BLOCK
    slot_tok = jnp.full((n_slots,), t, jnp.int32).at[dest].set(t_s)
    slot_w = jnp.zeros((n_slots,), jnp.float32).at[dest].set(w_s)
    blk_e = jnp.minimum(jnp.searchsorted(pend, jnp.arange(n_blocks, dtype=jnp.int32) * MOE_BLOCK, side='right'), N_EXPERTS - 1)
    x_pad = jnp.concatenate([xt, jnp.zeros((1, D_MODEL), xt.dtype)], axis=0)

    def run_block(args):
        e, toks, w = args
        xb = x_pad[toks]
        h = jax.nn.silu(xb @ w_gate[e]) * (xb @ w_up[e])
        return (h @ w_down[e]) * w[:, None].astype(xb.dtype)

    yb = lax.map(run_block, (blk_e, slot_tok.reshape(n_blocks, MOE_BLOCK), slot_w.reshape(n_blocks, MOE_BLOCK)))
    y = jnp.zeros((t + 1, D_MODEL), xt.dtype).at[slot_tok].add(yb.reshape(n_slots, D_MODEL))[:t]
    return y.reshape(shp)

def _post_norm_block(x, mix, ln1_g, ln1_b, ln2_g, ln2_b, rwg, rbg, rwe, rbe, wg, wu, wd):
    h = _layernorm(DN_ALPHA * x + mix, ln1_g, ln1_b)
    return _layernorm(DN_ALPHA * h + _moe(h, rwg, rbg, rwe, rbe, wg, wu, wd), ln2_g, ln2_b)

def setup_inputs(seed: int = 0) -> dict:
    key = jax.random.key(seed)
    ks = jax.random.split(key, 32)
    n_pages = PAST_LEN // PAGE_SIZE
    n_used = DEC_BATCH * n_pages
    n_phys = n_used + n_used // 4
    L = DEPTH

    def nrm(k, shape, scale):
        return jax.random.normal(k, shape, jnp.float32) * scale

    page_table = jax.random.permutation(ks[5], n_phys)[:n_used].reshape(DEC_BATCH, n_pages).astype(jnp.int32)
    return {
        'x_prompt': nrm(ks[0], (BATCH, SEQ, D_MODEL), 1.0),
        'x_sample': nrm(ks[1], (DEC_BATCH, DEC_SEQ, D_MODEL), 1.0),
        'cache_ckv': nrm(ks[2], (L, n_phys, PAGE_SIZE, KV_LORA), 1.0),
        'cache_krope': nrm(ks[3], (L, n_phys, PAGE_SIZE, ROPE_DIM), 1.0),
        'state_conv': nrm(ks[4], (L, DEC_BATCH, CONV_W - 1, D_CONV), 0.5),
        'page_table': page_table,
        'w_in': nrm(ks[6], (L, D_MODEL, IN_COLS), D_MODEL ** -0.5),
        'conv_w': nrm(ks[7], (L, CONV_W, D_CONV), CONV_W ** -0.5),
        'q_norm_g': 1.0 + nrm(ks[8], (L, Q_LORA), 0.02),
        'w_uq': nrm(ks[9], (L, Q_LORA, N_HEADS * QK_DIM), Q_LORA ** -0.5),
        'kv_norm_g': 1.0 + nrm(ks[10], (L, KV_LORA), 0.02),
        'w_uk': nrm(ks[11], (L, KV_LORA, N_HEADS, NOPE_DIM), KV_LORA ** -0.5),
        'w_uv': nrm(ks[12], (L, KV_LORA, N_HEADS, V_DIM), DN_BETA * KV_LORA ** -0.5),
        'w_br_conv': nrm(ks[13], (L, D_CONV, D_MODEL), DN_BETA * D_CONV ** -0.5),
        'w_br_attn': nrm(ks[14], (L, N_HEADS * V_DIM, D_MODEL), DN_BETA * (N_HEADS * V_DIM) ** -0.5),
        'w_o': nrm(ks[15], (L, D_MODEL, D_MODEL), DN_BETA * D_MODEL ** -0.5),
        'ln1_g': 1.0 + nrm(ks[16], (L, D_MODEL), 0.02),
        'ln1_b': nrm(ks[17], (L, D_MODEL), 0.02),
        'router_w_group': nrm(ks[18], (L, D_MODEL, N_GROUPS), D_MODEL ** -0.5),
        'router_b_group': nrm(ks[19], (L, N_GROUPS), 0.01),
        'router_w_expert': nrm(ks[20], (L, D_MODEL, N_EXPERTS), D_MODEL ** -0.5),
        'router_b_expert': nrm(ks[21], (L, N_EXPERTS), 0.01),
        'w_gate': nrm(ks[22], (L, N_EXPERTS, D_MODEL, D_EXPERT), D_MODEL ** -0.5),
        'w_up': nrm(ks[23], (L, N_EXPERTS, D_MODEL, D_EXPERT), DN_BETA * D_MODEL ** -0.5),
        'w_down': nrm(ks[24], (L, N_EXPERTS, D_EXPERT, D_MODEL), DN_BETA * D_EXPERT ** -0.5),
        'ln2_g': 1.0 + nrm(ks[25], (L, D_MODEL), 0.02),
        'ln2_b': nrm(ks[26], (L, D_MODEL), 0.02),
    }

def reference(x_prompt, x_sample, cache_ckv, cache_krope, state_conv, page_table,
              w_in, conv_w, q_norm_g, w_uq, kv_norm_g, w_uk, w_uv, w_br_conv, w_br_attn, w_o,
              ln1_g, ln1_b, router_w_group, router_b_group, router_w_expert, router_b_expert,
              w_gate, w_up, w_down, ln2_g, ln2_b):
    n_p, t_p, _ = x_prompt.shape
    n_s, t_s, _ = x_sample.shape
    past = page_table.shape[1] * PAGE_SIZE
    pos_p = jnp.arange(t_p)
    pos_s = past + jnp.arange(t_s)
    h_p, h_s = x_prompt, x_sample
    ckv_p, kr_p, cv_p, ckv_s, kr_s, cv_s = [], [], [], [], [], []
    for l in range(DEPTH):
        mix_w = (w_in[l], q_norm_g[l], w_uq[l], kv_norm_g[l])
        out_w = (conv_w[l], w_br_conv[l], w_br_attn[l], w_o[l])
        ffn_w = (ln1_g[l], ln1_b[l], ln2_g[l], ln2_b[l], router_w_group[l], router_b_group[l],
                 router_w_expert[l], router_b_expert[l], w_gate[l], w_up[l], w_down[l])
        b_g, u, q_nope, q_rope, ckv, kr, g_conv, g_attn = _in_proj(h_p, pos_p, *mix_w)
        u_ext = jnp.concatenate([jnp.zeros((n_p, CONV_W - 1, D_CONV), u.dtype), u], axis=1)
        o = _prompt_attention(q_nope, q_rope, ckv, kr, w_uk[l], w_uv[l])
        mix = _merge(b_g, u_ext, o, g_conv, g_attn, *out_w)
        h_p = _post_norm_block(h_p, mix, *ffn_w)
        ckv_p.append(ckv)
        kr_p.append(kr)
        cv_p.append(u_ext[:, -(CONV_W - 1):])
        b_g, u, q_nope, q_rope, ckv, kr, g_conv, g_attn = _in_proj(h_s, pos_s, *mix_w)
        u_ext = jnp.concatenate([state_conv[l].astype(u.dtype), u], axis=1)
        past_c = cache_ckv[l][page_table].reshape(n_s, past, KV_LORA)
        past_r = cache_krope[l][page_table].reshape(n_s, past, ROPE_DIM)
        o = _sample_attention(q_nope, q_rope, ckv, kr, past_c, past_r, w_uk[l], w_uv[l])
        mix = _merge(b_g, u_ext, o, g_conv, g_attn, *out_w)
        h_s = _post_norm_block(h_s, mix, *ffn_w)
        ckv_s.append(ckv)
        kr_s.append(kr)
        cv_s.append(u_ext[:, -(CONV_W - 1):])
    return (h_p, h_s, jnp.stack(ckv_p), jnp.stack(kr_p), jnp.stack(cv_p),
            jnp.stack(ckv_s), jnp.stack(kr_s), jnp.stack(cv_s))


_drawn_inputs = setup_inputs


def setup_inputs(seed=0):
    import zlib

    import numpy as np

    out = dict(_drawn_inputs(seed))
    spreads = {}
    factors = {'cache_ckv': 8.0,
     'cache_krope': 8.0,
     'q_norm_g': 8.0,
     'w_uq': 4.864,
     'kv_norm_g': 2.74,
     'w_uk': 4.938,
     'w_uv': 3.703,
     'w_br_attn': 3.692,
     'router_b_group': 39.938,
     'router_b_expert': 25.831,
     'ln2_g': 7.746,
     'ln2_b': 7.844}
    for name, (base, spread) in spreads.items():
        noise = np.random.default_rng([zlib.crc32(name.encode()), seed]).standard_normal(out[name].shape)
        drawn = base * np.exp(spread * noise) if base else spread * noise
        out[name] = __import__('jax').numpy.asarray(drawn.astype(out[name].dtype))
    for name, factor in factors.items():
        out[name] = (out[name] * factor).astype(out[name].dtype)
    return out
```

```python
from contextlib import ExitStack

import numpy as np

import concourse.bass as bass
from concourse import mybir

F32 = mybir.dt.float32
I32 = mybir.dt.int32
U32 = mybir.dt.uint32
ALU = mybir.AluOpType
ACT = mybir.ActivationFunctionType
AX_X = mybir.AxisListType.X
ds = bass.ds

P = 128
D = 1024
SEQ = 1024
NS = 8
T = SEQ + NS
NT = SEQ // P + 1
KD = D // P
DC = 512
NH = 8
QL_ = 384
CL = 256
NOPE, ROPE, VD = 64, 32, 64
QK = NOPE + ROPE
SCALE = QK ** -0.5
PAGE = 128
NPG = 32
RT = 8
NLD = NPG // RT
PAST = PAGE * NPG
NG, EG = 4, 8
NE = NG * EG
FE = 512
ALPHA = 2.0 ** 0.25
LN_EPS, RMS_EPS = 1e-5, 1e-6
NOVER = (2 * T - 1) // P
NBLK = NE + NOVER
SP3 = T // 3
NEG = -1e30

C_B, C_C, C_H = 0, DC, 2 * DC
C_Q = 3 * DC
C_KV = C_Q + QL_
C_KR = C_KV + CL
C_GC = C_KR + ROPE
C_GA = C_GC + D


def rows_of(t):
    return P if t < NT - 1 else NS


class Chain:

    def __init__(self, eng, sem):
        self.eng, self.sem, self.base, self.n = eng, sem, 0, 0

    def link(self, ins):
        self.n += 1
        ins.then_inc(self.sem, 1)
        self.eng.wait_ge(self.sem, self.base + self.n)

    def enter(self, i, per):
        self.base0, self.per, self.n0 = self.base + self.n, per, 0
        self.base, self.n = self.base0 + i * per, 0

    def leave(self, turns):
        assert self.n == self.per, (self.n, self.per)
        self.base, self.n = self.base0 + turns * self.per, 0


def build(nc, a):
    ctx = ExitStack()
    with ctx:
        def sem(name):
            return ctx.enter_context(nc.semaphore(name))

        arena = ctx.enter_context(nc.sbuf_tensor("arena", [P, 53200], F32))
        psum = ctx.enter_context(nc.psum_tensor("psum", [P, 8, 512], F32))
        ctx.enter_context(nc.allow_non_contiguous_dma(reason="small vectors laid out over partitions"))

        def at(off, *shape):
            n = int(np.prod(shape))
            v = arena[:, off:off + n]
            if len(shape) == 2:
                v = v.rearrange("p (a b) -> p a b", b=shape[1])
            if len(shape) == 3:
                v = v.rearrange("p (a b c) -> p a b c", b=shape[1], c=shape[2])
            return v

        class Zone:
            def __init__(self, lo, hi):
                self.o, self.hi = lo, hi

            def __call__(self, *shape):
                v = at(self.o, *shape)
                self.o += int(np.prod(shape))
                assert self.o <= self.hi, (self.o, self.hi)
                return v

        Z0, Z1, Z2, Z3, Z4, END = 0, 9216, 17472, 25664, 50240, 53200
        HALF_W = Z3 + 3 * KD * FE
        xT = at(Z0, KD, T)
        h_sb = at(Z0, NT, D)
        z = Zone(Z1, Z2)
        sq = z(5, T)
        rs = z(2, T)
        z = Zone(Z2, Z3)
        kr_tmp = z(2, T)
        x_in = z(3, D)
        z = Zone(Z3, Z4)
        convT = z(4, T)
        oT = z(4, T)
        wring = z(6, KD, P)
        ckvT = z(2, T)
        krT = z(T)
        cq_off = z.o
        cqT = z(3, T)
        cosT = z(T)
        sinT = z(T)
        free3 = z.o
        nat = z(2, CL + ROPE)
        z = Zone(Z1, Z2)
        v_sb = z(SEQ // P, NH, VD + 1)
        o_nat = z(SEQ // P, NH * VD)
        z = Zone(Z2, Z3)
        prob = z(SEQ)
        probT = z(SEQ // P, P)
        kT = z(2, SEQ)
        qT = z(2, T)
        wuq = z(3, P)
        wuk = z(2, NOPE)
        gate_st0 = z(T)
        gate_st = [gate_st0, at(free3 + 2 * (CL + ROPE), T)]
        ring45 = wring[:, 4:6, :, :].rearrange("p a b c -> p (a b) c")
        rope_tmp = ring45.rearrange("p a c -> p (a c)")[:, 0:T]
        wuk_all = cosT[:, 0:2 * NH * NOPE].rearrange("p (c n) -> p c n", c=2)
        wukT = sinT[:, 0:4 * CL].rearrange("p (i n) -> p i n", i=4)
        kn = [at(Z2, NLD, RT, CL), at(Z1, NLD, RT, CL)]
        kr_in = [at(cq_off + i * 1024, NLD, RT * ROPE) for i in range(2)]
        z = Zone(free3, Z4)
        kt_s = [z(9, P), ring45[:, 0:9, :]]
        s_prob = z(NH * (NPG + 1))
        s_self = z(3, NS * NH)
        s_max, s_all, s_top, s_sum, s_tot, s_rec, s_o = (z(NH) for _ in range(7))
        z = Zone(cq_off + 2048, free3)
        c_sb = z(T)
        u_sb = z(T + 2)
        acc = z(T)
        z = Zone(cq_off, free3)
        gate_in = z(4, T)
        mT = at(Z1, KD, T)
        wo_sb = at(Z2, KD, D)
        z = Zone(HALF_W, Z4)
        xr = z(3, D)
        ln_t = z(2, D)
        ln1g, ln1b = z(D), z(D)
        hT = z(2, KD, P)
        w_r = z(KD, NG + NE)
        r_pos, r_d, r_t = z(NT, NE), z(NT, NE), z(NT, NE)
        iota_i, iota_f = z(P), z(P)
        oh_row = xr.rearrange("p a d -> p (a d)")[:, 0:2 * NT * P].rearrange("p (n c) -> p n c", c=P)
        oh_blk = ln_t.rearrange("p a d -> p (a d)")[:, 0:2 * NT * NBLK].rearrange("p (n c) -> p n c", c=NBLK)
        extra, skip, ob = z(NE), z(NE), z(2, NE)
        o_cmp = z(NOVER, NE)
        row_i2, blk_i = z(2, NT), z(2, NT)
        row_f2, blk_f = z(2, NT), z(2, NT)
        z = Zone(Z3, Z4)
        we = [(z(KD, FE), z(KD, FE), z(4, D)) for _ in range(2)]
        z = Zone(Z1, Z3)
        xg = z(2, D)
        xgT = z(2, KD, P)
        sig = z(FE)
        act_t = z(FE)
        hid = z(2, FE)
        hhT = z(2, 4, P)
        yo = z(2, D)
        z = Zone(HALF_W, Z4)
        y1, y2 = z(3, D), z(3, D)
        fin = z(4, D)
        ln2g, ln2b = z(D), z(D)
        z = Zone(Z4, END)
        ident = z(P)
        ones = z(P)
        tri = z(P)
        small = z.o
        mask = z(P)
        qg = z(3)
        kvg = z(2)
        cw = z(4, 3)
        st_nat = z(DC)
        uend_nat = st_nat
        sel = st_nat[0:RT, 0:P]
        pt_i = st_nat[0:RT, P:P + 32]
        pt_f = st_nat[0:RT, P + 32:P + 64]
        row_i = st_nat[:, P + 64:P + 65]
        row_f = st_nat[:, P + 65:P + 66]
        stT = z(4, 16)
        uend = z(4, 10)
        w_uv = z(2, NH * VD)
        cache_idx = z(NS * NLD)
        q_bd = z(4, 2, NS)
        q_lat = z(2, NS, NH)
        q_rot = z(NS, 4, NH)
        o_lat = z(2, NS, NH)
        self_s = z(NS * NH)
        a_max = z(8)
        a_neg = z(8)
        a_rec = z(8)
        z = Zone(small, END)
        m1, m2, m12 = z(NT, NE), z(NT, NE), z(NT, NE)
        cum = z(NT + 1, NE)
        egroup = z(NE)
        r_bias = z(NG + NE)
        lg, le, lem = z(8), z(NE), z(NE)
        g8, g8i, t8, t8i = z(8), z(8), z(8), z(8)
        chosen = z(3)
        gx = z(NT, 8)
        rsm = z(2, 4)
        bst = z(2, 6)
        mv = z(2, 2)
        wts, p_sum = z(2, NT), z(NT)
        d_f, slot_of = z(2, NT), z(2, NT)
        tok_i, tok_f = z(NT), z(NT)
        blk_tok = z(NBLK)
        ov_f, ov_e, ov_on = z(NOVER), z(NOVER), z(NOVER)

        consts_in = sem("consts_in")
        pool_const = sem("pool_const")
        x_ld = [sem(f"x_ld{i}") for i in range(3)]
        xt_done = sem("xt_done")
        xt_act, xt_dve = sem("xt_act"), sem("xt_dve")
        w_ld = [sem(f"w_ld{i}") for i in range(6)]
        proj_done = sem("proj_done")
        setev = [sem("setev0"), sem("setev1")]
        sq_ready = sem("sq_ready")
        std_ready = sem("std_ready")
        norm_ready = sem("norm_ready")
        st_done = sem("st_done")
        st_ready = sem("st_ready")
        dve_chain = sem("dve_chain")
        nat_done = sem("nat_done")
        nat_ev = sem("nat_ev")
        NAT_OUT = [32 * ((NT - q + 1) // 2) for q in range(2)]
        nat_out = [sem("nat_out0"), sem("nat_out1")]
        ue_done, ue_ev, ue_out = sem("ue_done"), sem("ue_ev"), sem("ue_out")
        pass_out = sem("pass_out")

        wuq_ld, wuk_ld = sem("wuq_ld"), sem("wuk_ld")
        wuv_ld = sem("wuv_ld")
        wgate_ld = [sem(f"wgate_ld{i}") for i in range(4)]
        pool_v = sem("pool_v")
        v_done, v_act = sem("v_done"), sem("v_act")
        q_done, k_done = sem("q_done"), sem("k_done")
        fill_done = sem("fill_done")
        fill_act = sem("fill_act")
        q_dve, k_act = sem("q_dve"), sem("k_act")
        qs_dve = sem("qs_dve")
        s_done, max_dve, exp_act = sem("s_done"), sem("max_dve"), sem("exp_act")
        pt_done, pt_act, pt_dve = sem("pt_done"), sem("pt_act"), sem("pt_dve")
        pv_done, o_dve = sem("pv_done"), sem("o_dve")
        gate_out = [sem("gate_out0"), sem("gate_out1")]
        ot_done, ot_act, ot_dve = sem("ot_done"), sem("ot_act"), sem("ot_dve")
        pool_sel, idx_i, idx_done, idx_ready = sem("pool_sel"), sem("idx_i"), sem("idx_done"), sem("idx_ready")
        idx_f = sem("idx_f")
        wt_done, wt_dve, ql_done = sem("wt_done"), sem("wt_dve"), sem("ql_done")
        ss_dve, self_done, self_dve = sem("ss_dve"), sem("self_done"), sem("self_dve")
        kn_ld = [[sem(f"kn_ld{p}{g}") for g in range(NLD)] for p in range(2)]
        kt_done, kt_act, kt_dve = sem("kt_done"), sem("kt_act"), sem("kt_dve")
        sc_done, smax_dve, smax_pool, sx_dve, sp_act, ssum_dve = (sem(n) for n in ("sc_done", "smax_dve", "smax_pool", "sx_dve", "sp_act", "ssum_dve"))
        spv_done, ol_dve = sem("spv_done"), sem("ol_dve")
        wconv_ld = [sem(f"wconv_ld{i}") for i in range(3)]
        cfill_done, c_act, cu_dve = sem("cfill_done"), sem("c_act"), sem("cu_dve")
        os_done, os_dve = sem("os_done"), sem("os_dve")
        gate_ld, GATE_BASE = w_ld, (16, 16, 48, 16)
        sg_act = sem("sg_act")
        y_done, yc_dve, ya_dve, m_dve = sem("y_done"), sem("yc_dve"), sem("ya_dve"), sem("m_dve")
        ln1_ld = sem("ln1_ld")
        wo_done, r_dve, var_dve, sd_act = sem("wo_done"), sem("r_dve"), sem("var_dve"), sem("sd_act")
        h_dve, h_out = sem("h_dve"), sem("h_out")
        ht_done, ht_act, lg_done, lg_dve = sem("ht_done"), sem("ht_act"), sem("lg_done"), sem("lg_dve")
        pool_rt, sel_dve, gx_act = sem("pool_rt"), sem("sel_dve"), sem("gx_act")
        pos_done, oh_dve, tb_done, blk_dve = sem("pos_done"), sem("oh_dve"), sem("tb_done"), sem("blk_dve")
        we_ld = [[sem(f"we_ld{p}{m}") for m in range(3)] for p in range(2)]
        xg_ld = [sem("xg_ld0"), sem("xg_ld1")]
        te_done, te_act, te_dve = sem("te_done"), sem("te_act"), sem("te_dve")
        g_done, u_done, gs_act, gm_dve, hu_dve = sem("g_done"), sem("u_done"), sem("gs_act"), sem("gm_dve"), sem("hu_dve")
        th_done, th_act, d_done, y_act, y_dve = sem("th_done"), sem("th_act"), sem("d_done"), sem("y_act"), sem("y_dve")
        y_out = [sem("y_out0"), sem("y_out1")]
        ow_ld, ox_ld, ov_out, fill_out = sem("ow_ld"), sem("ox_ld"), sem("ov_out"), sem("fill_out")
        wt_rdy = sem("wt_rdy")
        y1_act, sum_dve, nb_dve, n_act = sem("y1_act"), sem("sum_dve"), sem("nb_dve"), sem("n_act")
        g_dve, f_pool = sem("g_dve"), sem("f_pool")
        yg_ld, YG_BASE = xg_ld + kn_ld[0][0:1], [16 * (NE // 2)] * 2 + [32 * (NS // 2)]
        f_out, F_BASE = nat_out + y_out, NAT_OUT + [16 * (NE // 2)] * 2

        gates = nc.dram_tensor("gates", (KD, 2, P, T), F32).ap()
        h_rows = nc.dram_tensor("h_rows", (T, D), F32).ap()
        y_slots = nc.dram_tensor("y_slots", (NBLK * P, D), F32).ap()
        block = ctx.enter_context(nc.Block())
        NQ = SEQ // P
        scores_ps = psum[:, 0:2, :].rearrange("p b n -> p (b n)")
        FB = 2
        def fill_ps(rows=P, lo=0):
            return psum[lo:lo + rows, FB:FB + 3, 0:SP3]
        SHARES = [(0, 0, 5), (0, 5, 10), (0, 10, 13), (0, 13, 16), (0, 16, 20), (0, 20, 24),
                  (1, 0, 3), (1, 3, 6), (1, 6, 8), (1, 8, 11), (1, 11, 13), (1, 13, 16), (1, 16, 18), (1, 18, 21),
                  (1, 21, 22), (1, 22, 24)]
        w_in = a["w_in"][0].rearrange("(k p) n -> p k n", p=P)

        OH = NT // 3
        NPRE, SUM_KV, SUM_Q = 8, 3, 7
        third = lambda v: v.rearrange("p (b n) -> p b n", n=SP3)
        def bset(s, rows=P, lo=0):
            return psum[lo:lo + rows, 3 * s:3 * s + 3, 0:SP3]

        @block.sync
        def _(sp):
            def load_x(t):
                r = rows_of(t)
                if t >= 3:
                    sp.wait_ge(xt_done, 2 * (t - 2))
                src = a["x_prompt"][0, t * P:(t + 1) * P, :] if t < NT - 1 else a["x_sample"][:, 0, :]
                sp.dma_start(x_in[0:r, t % 3, :], src).then_inc(x_ld[t % 3], 16)

            for t in range(2):
                load_x(t)

            def load_w(slot, col, n=P, at_=0):
                sp.dma_start(wring[:, slot, :, at_:at_ + n], w_in[:, :, col:col + n]).then_inc(w_ld[slot], 16)

            load_w(0, C_KV)
            load_w(1, C_KV + P)
            for t in range(2, NT):
                load_x(t)
            load_w(2, C_KR, ROPE)
            load_w(2, C_KR + 16, 16, ROPE)
            load_w(2, C_KR, 16, ROPE + 16)
            for j in range(3):
                load_w(3 + j, C_Q + j * P)
            sp.dma_start(a["new_conv_sample"][0, :, 0, :], a["state_conv"][0, :, 1, :]).then_inc(pass_out, 16)
            sp.dma_start(w_uv, a["w_uv"][0].rearrange("(c p) h d -> p c (h d)", p=P)).then_inc(wuv_ld, 16)
            w_uq = a["w_uq"][0].rearrange("(c p) n -> p c n", p=P)
            w_uk = a["w_uk"][0].rearrange("(c p) h d -> p c (h d)", p=P)

            def load_head(h):
                sp.dma_start(wuq[:, :, 0:QK], w_uq[:, :, ds(h * QK, QK)]).then_inc(wuq_ld, 16)
                sp.dma_start(wuq[:, :, QK:QK + 16], w_uq[:, :, ds(h * QK + NOPE + 16, 16)]).then_inc(wuq_ld, 16)
                sp.dma_start(wuq[:, :, QK + 16:P], w_uq[:, :, ds(h * QK + NOPE, 16)]).then_inc(wuq_ld, 16)
                sp.dma_start(wuk[:, :, :], w_uk[:, :, ds(h * NOPE, NOPE)]).then_inc(wuk_ld, 16)

            def load_gates(h, par):
                for g, col in enumerate((C_GC, C_GA)):
                    sp.dma_start(wring[:, 2 * par + g, :, :], w_in[:, :, ds(col + h * P, P)]).then_inc(wgate_ld[2 * par + g], 16)

            def store_gates(h):
                for g in range(2):
                    sp.wait_ge(fill_act, 3 * h + 2 + g)
                    sp.dma_start(gates[ds(h, 1), g, :, :].rearrange("a p n -> (a p) n"), gate_st[g]).then_inc(gate_out[g], 16)

            load_head(0)
            sp.wait_ge(proj_done, 2)
            load_gates(0, 0)
            for t in range(NT):
                r = rows_of(t)
                sp.wait_ge(nat_ev, t + 1)
                if t < NT - 1:
                    o1, o2 = a["new_ckv_prompt"][0, 0, t * P:t * P + r, :], a["new_krope_prompt"][0, 0, t * P:t * P + r, :]
                else:
                    o1, o2 = a["new_ckv_sample"][0, :, 0, :], a["new_krope_sample"][0, :, 0, :]
                sp.dma_start(o1, nat[0:r, t % 2, 0:CL]).then_inc(nat_out[t % 2], 16)
                sp.dma_start(o2, nat[0:r, t % 2, CL:CL + ROPE]).then_inc(nat_out[t % 2], 16)
            with sp.Fori(0, NH // 2 - 1) as i:
                for par in range(2):
                    h = 2 * i + par
                    sp.wait_ge(k_done, h + 1)
                    load_head(h + 1)
                    load_gates(h + 1, 1 - par)
                    store_gates(h)
            sp.wait_ge(k_done, NH - 1)
            load_head(NH - 1)
            load_gates(NH - 1, 1)
            store_gates(NH - 2)
            store_gates(NH - 1)
            sp.wait_ge(q_dve, NH)
            sp.dma_start(wuk_all, w_uk).then_inc(wuk_ld, 16)
            with sp.Fori(0, 4) as j:
                for u, col in enumerate((C_C, C_H, C_B)):
                    sp.wait_ge(fill_done, 2 * NH)
                    sp.wait_ge(cfill_done, 3 * j)
                    sp.dma_start(wring[:, u, :, :], w_in[:, :, ds(col + j * P, P)]).then_inc(wconv_ld[u], 16)
            w_bc = a["w_br_conv"][0].rearrange("(k p) n -> p k n", p=P)
            w_ba = a["w_br_attn"][0].rearrange("(k p) n -> p k n", p=P)

            def load_branch(j, par):
                for g, w in enumerate((w_bc, w_ba)):
                    sp.dma_start(wring[:, 2 * par + g, 0:4, :], w[:, :, ds(j * P, P)]).then_inc(wgate_ld[2 * par + g], 16)
                    sp.dma_start(gate_in[:, 2 * par + g, :], gates[ds(j, 1), g, :, :].rearrange("a p n -> (a p) n")).then_inc(gate_ld[2 * par + g], 16)

            for q in range(2):
                sp.wait_ge(gate_out[q], 16 * NH)
            sp.wait_ge(cfill_done, 12)
            sp.wait_ge(cu_dve, 8)
            sp.wait_ge(ol_dve, NS)
            for par in range(2):
                load_branch(par, par)
            sp.dma_start(wo_sb, a["w_o"][0].rearrange("(k p) n -> p k n", p=P)).then_inc(wuv_ld, 16)
            with sp.Fori(0, KD // 2 - 1) as i:
                for par in range(2):
                    sp.wait_ge(m_dve, 2 * i + par + 1)
                    load_branch(2 * i + par + 2, par)
            sp.wait_ge(ue_ev, 1)
            sp.dma_start(a["new_conv_prompt"][0, 0, :, :], uend_nat[0:2, :]).then_inc(ue_out, 16)
            sp.dma_start(a["new_conv_sample"][0, :, 1, :], uend_nat[2:10, :]).then_inc(ue_out, 16)
            sp.wait_ge(m_dve, KD)

            def load_residual(t):
                src = a["x_prompt"][0, t * P:(t + 1) * P, :] if t < NT - 1 else a["x_sample"][:, 0, :]
                sp.dma_start(xr[0:rows_of(t), t % 3, :], src).then_inc(x_ld[t % 3], 16)

            for t in range(3):
                load_residual(t)
            rw = lambda n: a[n][0].rearrange("(k p) n -> p k n", p=P)
            sp.dma_start(ln1g, a["ln1_g"][0].partition_broadcast(P)).then_inc(ln1_ld, 16)
            sp.dma_start(ln1b, a["ln1_b"][0].partition_broadcast(P)).then_inc(ln1_ld, 16)
            sp.dma_start(w_r[:, :, 0:NG], rw("router_w_group")).then_inc(ln1_ld, 16)
            sp.dma_start(w_r[:, :, NG:NG + NE], rw("router_w_expert")).then_inc(ln1_ld, 16)
            sp.dma_start(r_bias[:, 0:NG], a["router_b_group"][0].partition_broadcast(P)).then_inc(ln1_ld, 16)
            sp.dma_start(r_bias[:, NG:NG + NE], a["router_b_expert"][0].partition_broadcast(P)).then_inc(ln1_ld, 16)

            def weights(e):
                one = lambda n: a[n][0, ds(e, 1)].rearrange("o (k p) n -> p (o k) n", p=P)
                return one("w_gate"), one("w_up"), one("w_down")

            def load_expert(e, par, used=True):
                for m, w in enumerate(weights(e)):
                    if used:
                        sp.wait_ge((g_done, u_done, d_done)[m], e - 1)
                    sp.dma_start(we[par][m], w).then_inc(we_ld[par][m], 16)

            load_expert(0, 0, used=False)
            for t in range(NT):
                sp.wait_ge(h_dve, t + 1)
                sp.dma_start(h_rows[t * P:t * P + rows_of(t), :], h_sb[0:rows_of(t), t, :]).then_inc(h_out, 16)
                if t + 3 < NT:
                    load_residual(t + 3)
            sp.wait_ge(blk_dve, 1)
            for q in range(2):
                sp.wait_ge(xg_ld[q], 16)
            load_expert(1, 1, used=False)
            with sp.Fori(0, NE // 2 - 1) as i:
                for par in range(2):
                    load_expert(2 * i + 2 + par, par)
            sp.wait_ge(d_done, NE)
            sp.dma_start(ln2g, a["ln2_g"][0].partition_broadcast(P)).then_inc(ln1_ld, 16)
            sp.dma_start(ln2b, a["ln2_b"][0].partition_broadcast(P)).then_inc(ln1_ld, 16)
            with sp.If(sp.value_load(ov_on[0:1, 0:1].bitcast(I32), min_val=0, max_val=1)):
                with sp.Fori(0, NOVER) as o:
                    on = sp.value_load(ov_on[0:1, ds(o, 1)].bitcast(I32), min_val=0, max_val=1)
                    with sp.If(on):
                        e = sp.value_load(ov_e[0:1, ds(o, 1)].bitcast(I32), min_val=0, max_val=NE - 1)
                        sp.wait_ge(d_done, NE + o)
                        for m, w in enumerate(weights(e)):
                            sp.dma_start(we[0][m], w).then_inc(ow_ld, 16)
            for t in range(NT):
                sp.wait_ge(f_pool, t + 1)
                dst = a["y_prompt"][0, t * P:(t + 1) * P, :] if t < NT - 1 else a["y_sample"][:, 0, :]
                sp.dma_start(dst, fin[0:rows_of(t), t % 4, :]).then_inc(f_out[t % 4], 16)
            sp.wait_ge(h_out, 16 * NT)
            sp.wait_ge(ue_out, 32)
            sp.wait_ge(pass_out, 16)
            for q in range(2):
                sp.wait_ge(nat_out[q], NAT_OUT[q])
            for q in range(4):
                sp.wait_ge(f_out[q], F_BASE[q] + 16 * ((NT - q + 3) // 4))
            for q in range(2):
                sp.wait_ge(gate_out[q], 16 * NH)

        N_CONST, NPC = 8, 9

        @block.gpsimd
        def _(pool):
            pool.memset(ident, 0.0).then_inc(pool_const, 1)
            pool.memset(ones, 1.0).then_inc(pool_const, 1)
            pool.memset(mask, 0.0).then_inc(pool_const, 1)
            pool.memset(q_rot, 0.0).then_inc(pool_const, 1)
            pool.memset(q_bd, 0.0).then_inc(pool_const, 1)
            pool.memset(tri, 1.0).then_inc(pool_const, 1)
            pool.wait_ge(pool_const, 6)
            pool.affine_select(out=ident, in_=ident, compare_op=ALU.not_equal, fill=1.0, base=0,
                               pattern=[[-1, P]], channel_multiplier=1).then_inc(pool_const, 1)
            pool.affine_select(out=mask, in_=mask, compare_op=ALU.is_ge, fill=NEG, base=0,
                               pattern=[[-1, P]], channel_multiplier=1).then_inc(pool_const, 1)
            pool.affine_select(out=tri, in_=tri, compare_op=ALU.is_gt, fill=0.0, base=0,
                               pattern=[[1, P]], channel_multiplier=-1).then_inc(pool_const, 1)
            pool.dma_start(st_nat[0:16, :], a["state_conv"][0].rearrange("b w c -> (b w) c")).then_inc(consts_in, 16)
            pool.dma_start(qg, a["q_norm_g"][0].rearrange("(c p) -> p c", p=P)).then_inc(consts_in, 16)
            pool.dma_start(kvg, a["kv_norm_g"][0].rearrange("(c p) -> p c", p=P)).then_inc(consts_in, 16)
            for k in range(3):
                pool.dma_start(cw[:, :, k], a["conv_w"][0, k].rearrange("(j p) -> p j", p=P)).then_inc(consts_in, 16)
            pool.wait_ge(xt_done, NT)
            pool.dma_start(cosT, a["cos_table"]).then_inc(consts_in, 16)
            pool.dma_start(sinT, a["sin_table"]).then_inc(consts_in, 16)
            pool.wait_ge(st_done, 1)
            pool.dma_start(pt_i.bitcast(I32), a["page_table"].rearrange("b (g q) -> q (b g)", q=RT)).then_inc(idx_i, 16)
            pool.memset(sel, 1.0).then_inc(pool_sel, 1)
            pool.iota(row_i.bitcast(I32), pattern=[[0, 1]], base=0, channel_multiplier=1).then_inc(pool_sel, 1)
            pool.wait_ge(pool_sel, 1)
            RW = P // RT
            pool.affine_select(out=sel, in_=sel, compare_op=ALU.is_ge, fill=0.0, base=0, pattern=[[1, P]], channel_multiplier=-RW).then_inc(pool_sel, 1)
            pool.wait_ge(pool_sel, 3)
            pool.affine_select(out=sel, in_=sel, compare_op=ALU.is_ge, fill=0.0, base=RW - 1, pattern=[[-1, P]], channel_multiplier=RW).then_inc(pool_sel, 1)

            pool.wait_ge(proj_done, NPRE)
            pool.memset(v_sb[:, :, :, VD:VD + 1], 1.0).then_inc(pool_v, 1)
            ckv_rows = a["cache_ckv"][0].rearrange("n (s r) c -> (n s) (r c)", r=RT)
            kr_rows = a["cache_krope"][0].rearrange("n (s r) c -> (n s) (r c)", r=RT)

            def load_cache(b):
                for g in range(NLD):
                    off = bass.IndirectOffsetOnAxis(ap=cache_idx[:, b * NLD + g:b * NLD + g + 1].bitcast(U32), axis=0)
                    pool.indirect_dma_start(kn[b % 2][:, g, :, :].rearrange("p r c -> p (r c)"), None, ckv_rows, off).then_inc(kn_ld[b % 2][g], 16)
                    pool.indirect_dma_start(kr_in[b % 2][:, g, :], None, kr_rows, off).then_inc(kn_ld[b % 2][g], 16)

            for o in range(NOVER):
                pool.wait_ge(k_done, o // 2 + 1)
                pool.dma_start(y_slots[(NE + o) * P:(NE + o + 1) * P, :], a["x_prompt"][0, 0:P, :]).then_inc(fill_out, 16)
            pool.wait_ge(idx_ready, 1)
            pool.wait_ge(o_dve, NQ * NH)
            pool.wait_ge(gate_out[0], 16 * NH)
            load_cache(0)
            pool.wait_ge(ot_done, NQ)
            load_cache(1)
            for b in range(NS):
                pool.wait_ge(smax_dve, b + 1)
                pool.partition_all_reduce(s_all, s_max, P, bass.bass_isa.ReduceOp.max).then_inc(smax_pool, 1)
                if b + 2 < NS:
                    pool.wait_ge(spv_done, b + 1)
                    load_cache(b + 2)
            pool.wait_ge(os_dve, 1)
            pool.wait_ge(ue_out, 32)
            pool.wait_ge(m_dve, KD)
            for v, c in ((m1, 0.0), (m2, 0.0), (m12, 0.0), (cum[:, 0, :], 0.0), (gx, 0.0), (lg, -3e38)):
                pool.memset(v, c).then_inc(pool_rt, 1)
            pool.iota(iota_i.bitcast(I32), pattern=[[1, P]], base=0, channel_multiplier=0).then_inc(pool_rt, 1)
            pool.iota(tok_i.bitcast(I32), pattern=[[P, NT]], base=0, channel_multiplier=1).then_inc(pool_rt, 1)

            def gather_block(blk, par, loaded):
                off = bass.IndirectOffsetOnAxis(ap=blk_tok[:, blk:blk + 1].bitcast(U32), axis=0)
                pool.indirect_dma_start(xg[:, par, :], None, h_rows, off).then_inc(loaded, 16)

            pool.wait_ge(blk_dve, 1)
            pool.wait_ge(h_out, 16 * NT)
            for e in range(NE):
                if e >= 2:
                    pool.wait_ge(te_done, e - 1)
                gather_block(e, e % 2, xg_ld[e % 2])
            pool.wait_ge(te_done, NE)
            with pool.If(pool.value_load(ov_on[0:1, 0:1].bitcast(I32), min_val=0, max_val=1)):
                for o in range(NOVER):
                    with pool.If(pool.value_load(ov_on[0:1, o:o + 1].bitcast(I32), min_val=0, max_val=1)):
                        if o > 0:
                            pool.wait_ge(te_done, NE + o)
                        gather_block(NE + o, 0, ox_ld)
                        pool.wait_ge(ov_out, 16 * o + 16)
                pool.wait_ge(blk_dve, 1)
            pool.wait_ge(fill_out, 16 * NOVER)
            for q in range(2):
                pool.wait_ge(y_out[q], 16 * (NE // 2))
            for t in range(NT + 3):
                if t < NT:
                    if t >= 3:
                        pool.wait_ge(sum_dve, t - 2)
                    r = rows_of(t)
                    for k, y in enumerate((y1, y2)):
                        off = bass.IndirectOffsetOnAxis(ap=slot_of[0:r, k, t:t + 1].bitcast(U32), axis=0)
                        pool.indirect_dma_start(y[0:r, t % 3, :], None, y_slots, off).then_inc(yg_ld[t % 3], 16)
                if t >= 3:
                    r = rows_of(t - 3)
                    v = fin[0:r, (t - 3) % 4, :]
                    pool.wait_ge(g_dve, t - 2)
                    pool.tensor_tensor(v, v, ln2b[0:r], ALU.add).then_inc(f_pool, 1)

        @block.tensor
        def _(pe):
            mm = nc.tensor.matmul
            pe.wait_ge(pool_const, NPC)
            for t in range(NT):
                r = rows_of(t)
                pe.wait_ge(x_ld[t % 3], 16 * (t // 3 + 1))
                for g in range(2):
                    if t >= 2:
                        pe.wait_ge((xt_act, xt_dve)[g], t - 1)
                    for k in range(4):
                        ins = nc.tensor.transpose(psum[:, 2 * (t % 2) + g, k * P:k * P + r],
                                                  x_in[0:r, t % 3, (4 * g + k) * P:(4 * g + k + 1) * P],
                                                  ident[0:r, 0:r])
                    ins.then_inc(xt_done, 1)
            pe.wait_ge(xt_act, NT)
            pe.wait_ge(xt_dve, NT)

            def project(s, slot, m=P):
                for k in range(KD):
                    for b in range(3):
                        ins = mm(psum[0:m, 3 * s + b, 0:SP3], wring[:, slot, k, 0:m],
                                 xT[:, k, b * SP3:(b + 1) * SP3], start=(k == 0), stop=(k == KD - 1))
                ins.then_inc(proj_done, 1)

            def square_sums(s, lo, hi):
                pe.wait_ge(sq_ready, hi)
                for k in range(lo, hi):
                    for b in range(3):
                        ins = mm(psum[:, 3 * s + b, 0:SP3], ones, sq[:, k, b * SP3:(b + 1) * SP3], start=(k == lo), stop=(k == hi - 1))
                ins.then_inc(proj_done, 1)

            for n in range(NPRE):
                if n >= 2:
                    pe.wait_ge(setev[n % 2], n // 2)
                if n in (SUM_KV, SUM_Q):
                    square_sums(n % 2, *((0, 2) if n == SUM_KV else (2, 5)))
                else:
                    slot = n if n < SUM_KV else n - 1
                    pe.wait_ge(w_ld[slot], 48 if slot == 2 else 16)
                    project(n % 2, slot, 2 * ROPE if slot == 2 else P)
                if n == SUM_KV:
                    pe.wait_ge(consts_in, 16 * N_CONST)
                    for j in range(4):
                        ins = nc.tensor.transpose(psum[:, 6, j * 16:(j + 1) * 16], st_nat[0:16, j * P:(j + 1) * P], ident[0:16, 0:16])
                    ins.then_inc(st_done, 1)
                if n == SUM_KV + 2:
                    pe.wait_ge(pool_sel, 4)
                    pe.wait_ge(idx_f, 1)
                    mm(psum[:, 7, 0:NS * NLD], sel, pt_f, start=True, stop=True).then_inc(idx_done, 1)
            pe.wait_ge(norm_ready, 1)
            pe.wait_ge(wuv_ld, 16)
            pe.wait_ge(setev[0], NPRE // 2)
            pe.wait_ge(idx_ready, 1)
            for t in range(NT):
                r = rows_of(t)
                if t < NQ:
                    if t >= 2:
                        pe.wait_ge(v_act, t - 1)
                    for c in range(2):
                        ins = mm(psum[:, t % 2, :], ckvT[:, c, t * P:(t + 1) * P], w_uv[:, c, :], start=(c == 0), stop=(c == 1))
                    ins.then_inc(v_done, 1)
                if t >= 2:
                    pe.wait_ge(nat_ev, t - 1)
                for c in range(2):
                    nc.tensor.transpose(psum[0:r, 6 + t % 2, c * P:(c + 1) * P], ckvT[:, c, t * P:t * P + r], ident)
                nc.tensor.transpose(psum[0:r, 6 + t % 2, CL:CL + ROPE], krT[0:ROPE, t * P:t * P + r],
                                    ident[0:ROPE, 0:ROPE]).then_inc(nat_done, 1)
            pe.wait_ge(nat_ev, NT)
            pe.wait_ge(setev[1], NPRE // 2)
            pe.wait_ge(norm_ready, 2)
            pe.wait_ge(v_act, NQ)
            pe.wait_ge(pool_v, 1)

            def project_head(h):
                pe.wait_ge(wuq_ld, 48 * h + 48)
                pe.wait_ge(fill_act, 3 * h)
                for k in range(3):
                    for b in range(3):
                        ins = mm(psum[:, FB + b, 0:SP3], wuq[:, k, :], cqT[:, k, b * SP3:(b + 1) * SP3], start=(k == 0), stop=(k == 2))
                ins.then_inc(q_done, 1)
                pe.wait_ge(wuk_ld, 16 * h + 16)
                for k in range(2):
                    for b in range(2):
                        ins = mm(psum[0:NOPE, b, :], wuk[:, k, :], ckvT[:, k, b * 512:(b + 1) * 512], start=(k == 0), stop=(k == 1))
                ins.then_inc(k_done, 1)

            def head(h, par, last):
                def fill(n):
                    g, lo, hi = SHARES[n]
                    slot = 2 * par + g
                    if lo == 0:
                        pe.wait_ge(wgate_ld[slot], 8 * (h - par) + 16)
                        pe.wait_ge(fill_act, 3 * h + 1 + g)
                    for u in range(lo, hi):
                        k, b = u // 3, u % 3
                        ins = mm(psum[:, FB + b, 0:SP3], wring[:, slot, k, :], xT[:, k, b * SP3:(b + 1) * SP3], start=(k == 0), stop=(k == KD - 1))
                    if hi == 3 * KD:
                        ins.then_inc(fill_done, 1)

                def scores(i):
                    L = (i + 1) * P
                    for b in range(0, L, 512):
                        w = min(512, L - b)
                        ins = mm(psum[:, b // 512, 0:w], qT[0:QK, par, i * P:(i + 1) * P], kT[0:QK, par, b:b + w], start=True, stop=True)
                    ins.then_inc(s_done, 1)

                def turn(i):
                    pe.wait_ge(exp_act, NQ * h + i + 1)
                    for k in range(i + 1):
                        ins = nc.tensor.transpose(psum[:, 5 + k // 4, k % 4 * P:(k % 4 + 1) * P], prob[:, k * P:(k + 1) * P], ident)
                    ins.then_inc(pt_done, 1)

                def values(i):
                    pe.wait_ge(pt_act, NQ * h + i + 1)
                    if i >= 4:
                        pe.wait_ge(pt_dve, NQ // 2 * h + i - 3)
                    pe.wait_ge(o_dve, NQ * h + i)
                    for k in range(i + 1):
                        ins = mm(psum[:, 7, 0:VD + 1], probT[:, k, :], v_sb[:, k, ds(h, 1), :].rearrange("p a d -> p (a d)"), start=(k == 0), stop=(k == i))
                    ins.then_inc(pv_done, 1)

                fill(0)
                pe.wait_ge(q_dve, h + 1)
                pe.wait_ge(k_act, h + 1)
                scores(0)
                fill(1)
                for i in range(NQ):
                    turn(i)
                    if i + 1 < NQ:
                        scores(i + 1)
                        fill(2 * i + 2)
                    elif not last:
                        project_head(h + 1)
                    values(i)
                    if i + 1 < NQ:
                        fill(2 * i + 3)

            project_head(0)
            with pe.Fori(0, NH // 2 - 1) as i:
                for par in range(2):
                    head(2 * i + par, par, False)
            head(NH - 2, 0, False)
            head(NH - 1, 1, True)
            pe.wait_ge(o_dve, NQ * NH)
            for t in range(NQ):
                if t >= 2:
                    pe.wait_ge((ot_act, ot_dve)[t % 2], t // 2)
                for c in range(4):
                    ins = nc.tensor.transpose(psum[:, t % 2, c * P:(c + 1) * P], o_nat[:, t, c * P:(c + 1) * P], ident)
                ins.then_inc(ot_done, 1)
            pe.wait_ge(wuk_ld, 16 * NH + 16)
            pe.wait_ge(fill_act, 3 * NH)
            for i in range(4):
                for c in range(2):
                    ins = nc.tensor.transpose(psum[:, 2 + i // 2, (i % 2) * CL + c * P:(i % 2) * CL + (c + 1) * P], wuk_all[:, c, i * P:(i + 1) * P], ident)
            ins.then_inc(wt_done, 1)
            pe.wait_ge(wt_dve, 1)
            pe.wait_ge(qs_dve, NH)
            for i in range(4):
                for c in range(2):
                    ins = mm(psum[:, 4, (2 * i + c) * 16:(2 * i + c + 1) * 16], wukT[:, i, c * P:(c + 1) * P],
                             q_bd[:, i, :, :].rearrange("p a b -> p (a b)"), start=True, stop=True)
            ins.then_inc(ql_done, 1)
            pe.wait_ge(ss_dve, 1)
            for c, r in ((0, P), (1, P), (2, ROPE)):
                ins = mm(psum[:, 4, 256:256 + NS * NH], ones[0:r, :], s_self[0:r, c, :], start=(c == 0), stop=(c == 2))
            ins.then_inc(self_done, 1)
            pe.wait_ge(self_dve, 1)
            pe.wait_ge(ot_act, NQ // 2)
            pe.wait_ge(ot_dve, NQ // 2)

            CUTS = [[0, 3, 5, 7, 9, 11, 13, 15, 17, 24, 38], [38, 41, 42, 43, 44, 45, 46, 47, 48, 57, 72]]
            AMONG = 2 * NPG - 12
            LATE = 5

            def sample(i, par):
                b = 2 * i + par

                def fill(lo, hi):
                    for m in range(lo, hi):
                        u, n = m // (3 * KD), m % (3 * KD)
                        if n == 0:
                            pe.wait_ge(wconv_ld[u], 16 * i + 16)
                            pe.wait_ge((cu_dve, c_act, cu_dve)[u], (2 * i, i + 1, 2 * i + 1)[u])
                        k, t = n // 3, n % 3
                        ins = mm(psum[:, FB + t, 0:SP3], wring[:, u, k, :], xT[:, k, t * SP3:(t + 1) * SP3], start=(k == 0), stop=(k == KD - 1))
                        if n == 3 * KD - 1:
                            ins.then_inc(cfill_done, 1)

                def key_scores(g, fill_from, fill_to):
                    o = g * 4 * NH
                    kt = kt_s[g % 2]
                    mm(psum[:, 6, o:o + 4 * NH], kt[:, 8, :], q_rot[:, ds(b, 1), :, :].rearrange("p a j h -> p (a j h)"), start=True, stop=False, skip_group_check=True)
                    for c in range(2):
                        if c:
                            fill(fill_from, fill_to)
                        for r in range(4):
                            ins = mm(psum[:, 6, o + r * NH:o + (r + 1) * NH], kt[:, 4 * c + r, :],
                                     q_lat[:, c, ds(b, 1), :].rearrange("p a h -> p (a h)"), start=False, stop=(c == 1), skip_group_check=True)
                    if g == 7:
                        ins.then_inc(sc_done, 1)

                for g in range(8):
                    G, r0 = g // 2, 4 * (g % 2)
                    if r0 == 0:
                        pe.wait_ge(kn_ld[par][G], 32 * i + 32)
                    pe.wait_ge(kt_act, 8 * b + g)
                    pe.wait_ge(kt_dve, 8 * b + g)
                    for c in range(2):
                        for r in range(4):
                            nc.tensor.transpose(psum[:, c, r * P:(r + 1) * P], kn[par][:, G, r0 + r, c * P:(c + 1) * P], ident)
                    nc.tensor.transpose(psum[:, 5, 0:P], kr_in[par][:, G, r0 * ROPE:(r0 + 4) * ROPE], ident).then_inc(kt_done, 1)
                    half_way = (CUTS[par][g] + CUTS[par][g + 1]) // 2
                    if g:
                        key_scores(g - 1, CUTS[par][g], half_way)
                        fill(half_way, CUTS[par][g + 1])
                    else:
                        fill(CUTS[par][g], CUTS[par][g + 1])
                pe.wait_ge(kt_act, 8 * b + 8)
                pe.wait_ge(kt_dve, 8 * b + 8)
                lo, hi = CUTS[par][9:11]
                key_scores(7, CUTS[par][8], CUTS[par][8] + 1 - par)
                fill(CUTS[par][8] + 1 - par, lo)
                pe.wait_ge(sp_act, b + 1)
                pe.wait_ge(ol_dve, b)
                for c in range(2):
                    for n in range(NPG):
                        q = c * NPG + n - LATE
                        if 0 <= q < AMONG:
                            fill(lo + -(-q * (hi - lo) // AMONG), lo + -(-(q + 1) * (hi - lo) // AMONG))
                        mm(psum[:, 7, c * NH:(c + 1) * NH], kn[par][:, n // RT, n % RT, c * P:(c + 1) * P], s_prob[:, n * NH:(n + 1) * NH],
                           start=(n == 0), stop=(n == NPG - 1))
                pe.wait_ge(ssum_dve, b + 1)
                mm(psum[:, 7, 2 * NH:3 * NH], ones, s_sum, start=True, stop=True).then_inc(spv_done, 1)

            with pe.Fori(0, NS // 2) as i:
                for par in range(2):
                    sample(i, par)
            pe.wait_ge(ol_dve, NS)
            for h in range(NH):
                for c in range(2):
                    ins = mm(psum[0:VD, 0, h * NS:(h + 1) * NS], w_uv[:, c, h * VD:(h + 1) * VD], o_lat[:, c, :, h], start=(c == 0), stop=(c == 1))
            ins.then_inc(os_done, 1)
            pe.wait_ge(cu_dve, 8)
            for j in range(4):
                ins = nc.tensor.transpose(psum[0:10, 1, j * P:(j + 1) * P], uend[:, j, :], ident)
            ins.then_inc(ue_done, 1)
            pe.wait_ge(os_dve, 1)
            pe.wait_ge(ue_ev, 1)
            with pe.Fori(0, KD // 2) as i:
                for par in range(2):
                    j = 2 * i + par
                    for g, (src, free) in enumerate(((convT, yc_dve), (oT, ya_dve))):
                        pe.wait_ge(wgate_ld[2 * par + g], 16 * (NH // 2) + 16 * i + 16)
                        pe.wait_ge(free, j)
                        for k in range(4):
                            for t in range(3):
                                ins = mm(psum[:, 3 * g + t, 0:SP3], wring[:, 2 * par + g, k, :], src[:, k, t * SP3:(t + 1) * SP3], start=(k == 0), stop=(k == 3))
                        ins.then_inc(y_done, 1)
            def out_proj(t):
                if t >= 2:
                    pe.wait_ge(r_dve, t - 1)
                r = rows_of(t)
                for k in range(KD):
                    for n in range(2):
                        ins = mm(psum[0:r, 2 * (t % 2) + n, :], mT[:, k, t * P:t * P + r], wo_sb[:, k, n * 512:(n + 1) * 512], start=(k == 0), stop=(k == KD - 1))
                ins.then_inc(wo_done, 1)

            def router(t):
                r = rows_of(t)
                pe.wait_ge(h_dve, t + 1)
                pe.wait_ge(ht_act, t)
                for k in range(KD):
                    ins = nc.tensor.transpose(psum[:, 4 + k // 4, (k % 4) * P:(k % 4) * P + r], h_sb[0:r, t, k * P:(k + 1) * P], ident[0:r, 0:r])
                ins.then_inc(ht_done, 1)
                pe.wait_ge(ht_act, t + 1)
                if t >= 2:
                    pe.wait_ge(lg_dve, t - 1)
                for k in range(KD):
                    ins = mm(psum[0:r, 6 + t % 2, 0:NG + NE], hT[:, t % 2, k, 0:r], w_r[:, k, :], start=(k == 0), stop=(k == KD - 1))
                ins.then_inc(lg_done, 1)

            pe.wait_ge(m_dve, KD)
            pe.wait_ge(wuv_ld, 32)
            out_proj(0)
            pe.wait_ge(ln1_ld, 96)
            for t in range(1, NT):
                out_proj(t)
                router(t - 1)
            router(NT - 1)
            pe.wait_ge(sel_dve, NT)
            every = lambda v: v.rearrange("p t e -> p (t e)")
            mm(psum[:, 0, 0:NT * NE], tri, every(m12), start=True, stop=False)
            mm(psum[:, 0, 0:NT * NE], ones, every(cum[:, 0:NT, :]), start=False, stop=True)
            mm(psum[:, 1, 0:NE], ones, cum[:, NT, :], start=True, stop=True).then_inc(pos_done, 1)
            for n in range(2 * NT):
                r = rows_of(n % NT)
                pe.wait_ge(oh_dve, n // OH + 1)
                ins = mm(psum[:, 2, 0:NBLK], oh_row[0:r, n, :], oh_blk[0:r, n, :], start=(n == 0), stop=(n == 2 * NT - 1))
            ins.then_inc(tb_done, 1)

            def turn_block(par):
                for k in range(KD):
                    ins = nc.tensor.transpose(psum[:, k // 4, (k % 4) * P:(k % 4 + 1) * P], xg[:, par, k * P:(k + 1) * P], ident)
                return ins

            def up(bank, w, xpar):
                for k in range(KD):
                    ins = mm(psum[:, bank, :], xgT[:, xpar, k, :], w[:, k, :], start=(k == 0), stop=(k == KD - 1))
                return ins

            def turn_hidden(par):
                for k in range(4):
                    ins = nc.tensor.transpose(psum[:, 4, k * P:(k + 1) * P], hid[:, par, k * P:(k + 1) * P], ident)
                return ins

            def down(w, par):
                for k in range(4):
                    for n in range(2):
                        ins = mm(psum[:, 5 + n, :], hhT[:, par, k, :], w[:, k, n * 512:(n + 1) * 512], start=(k == 0), stop=(k == 3))
                return ins

            def expert(e, half, par, first=False, last=False):
                pe.wait_ge(we_ld[par][0], 16 * half + 16)
                pe.wait_ge(te_act, e + 1)
                pe.wait_ge(te_dve, e + 1)
                pe.wait_ge(gm_dve, e)
                up(2, we[par][0], par).then_inc(g_done, 1)
                pe.wait_ge(we_ld[par][1], 16 * half + 16)
                pe.wait_ge(hu_dve, e)
                up(3, we[par][1], par).then_inc(u_done, 1)
                if not last:
                    pe.wait_ge(xg_ld[1 - par], 16 * (half + par) + 16)
                    turn_block(1 - par).then_inc(te_done, 1)
                if not first:
                    pe.wait_ge(we_ld[1 - par][2], 16 * (half + par - 1) + 16)
                    pe.wait_ge(th_act, e)
                    pe.wait_ge(y_act, e - 1)
                    pe.wait_ge(y_dve, e - 1)
                    down(we[1 - par][2], 1 - par).then_inc(d_done, 1)
                pe.wait_ge(hu_dve, e + 1)
                pe.wait_ge(th_act, e)
                turn_hidden(par).then_inc(th_done, 1)

            pe.wait_ge(blk_dve, 1)
            pe.wait_ge(xg_ld[0], 16)
            turn_block(0).then_inc(te_done, 1)
            expert(0, 0, 0, first=True)
            with pe.Fori(0, NE // 2 - 1) as i:
                expert(2 * i + 1, i, 1)
                expert(2 * i + 2, i + 1, 0)
            expert(NE - 1, NE // 2 - 1, 1, last=True)
            pe.wait_ge(we_ld[1][2], 16 * (NE // 2))
            pe.wait_ge(th_act, NE)
            pe.wait_ge(y_act, NE - 1)
            pe.wait_ge(y_dve, NE - 1)
            down(we[1][2], 1).then_inc(d_done, 1)
            pe.wait_ge(y_act, NE)
            pe.wait_ge(y_dve, NE)
            with pe.If(pe.value_load(ov_on[0:1, 0:1].bitcast(I32), min_val=0, max_val=1)):
                with pe.Fori(0, NOVER) as o:
                    on = pe.value_load(ov_on[0:1, ds(o, 1)].bitcast(I32), min_val=0, max_val=1)
                    with pe.If(on):
                        pe.wait_ge(ox_ld, 16 * o + 16)
                        pe.wait_ge(y_act, NE + o)
                        turn_block(0).then_inc(te_done, 1)
                        pe.wait_ge(te_act, NE + o + 1)
                        pe.wait_ge(ow_ld, 48 * o + 48)
                        up(2, we[0][0], 0).then_inc(g_done, 1)
                        up(3, we[0][1], 0).then_inc(u_done, 1)
                        pe.wait_ge(hu_dve, NE + o + 1)
                        turn_hidden(0).then_inc(th_done, 1)
                        pe.wait_ge(th_act, NE + o + 1)
                        down(we[0][2], 0).then_inc(d_done, 1)

        @block.scalar
        def _(act):
            for t in range(NT):
                r = rows_of(t)
                act.wait_ge(xt_done, 2 * t + 1)
                nc.scalar.copy(xT[:, 0:4, t * P:t * P + r],
                               psum[:, 2 * (t % 2), :].rearrange("p (k n) -> p k n", n=P)[:, :, 0:r]).then_inc(xt_act, 1)
            for k, dsts in enumerate((((0, ckvT[:, 0, :]), (1, ckvT[:, 1, :])), ((4, cqT[:, 0, :]), (5, cqT[:, 1, :]), (6, cqT[:, 2, :])))):
                for n, dst in dsts:
                    act.wait_ge(proj_done, n + 1)
                    nc.scalar.copy(third(dst), bset(n % 2)).then_inc(setev[n % 2], 1)
                act.wait_ge(setev[1], (SUM_KV, SUM_Q)[k] // 2 + 1)
                nc.scalar.activation(rs[:, k, :], rs[:, k, :], ACT.Sqrt).then_inc(std_ready, 1)
            for t in range(NT):
                r = rows_of(t)
                if t < NQ:
                    act.wait_ge(v_done, t + 1)
                    nc.scalar.copy(v_sb[:, t, :, 0:VD], psum[:, t % 2, :].rearrange("p (h d) -> p h d", d=VD)).then_inc(v_act, 1)
                act.wait_ge(nat_done, t + 1)
                if t >= 2:
                    act.wait_ge(nat_out[t % 2], 32 * (t // 2))
                nc.scalar.copy(nat[0:r, t % 2, :], psum[0:r, 6 + t % 2, 0:CL + ROPE]).then_inc(nat_ev, 1)

            def take_qk(h, par):
                act.wait_ge(q_done, h + 1)
                nc.scalar.copy(third(qT[:, par, :]), fill_ps()).then_inc(fill_act, 1)
                act.wait_ge(k_done, h + 1)
                nc.scalar.copy(kT[0:NOPE, par, :], scores_ps[0:NOPE, :]).then_inc(k_act, 1)

            def act_head(h, par, last):
                for i in range(NQ):
                    L = (i + 1) * P
                    act.wait_ge(max_dve, NQ * h + i + 1)
                    nc.scalar.activation(prob[:, 0:L], scores_ps[:, 0:L], ACT.Exp, bias=a_neg[:, i:i + 1], scale=SCALE).then_inc(exp_act, 1)
                    if i in (2, NQ - 1):
                        g = 0 if i == 2 else 1
                        act.wait_ge(fill_done, 2 * h + g + 1)
                        act.wait_ge(gate_out[g], 16 * h)
                        nc.scalar.copy(third(gate_st[g]), fill_ps()).then_inc(fill_act, 1)
                    act.wait_ge(pt_done, NQ * h + i + 1)
                    w = min(L, 512)
                    nc.scalar.copy(probT[:, 0:w // P, :].rearrange("p k n -> p (k n)"), psum[:, 5, 0:w]).then_inc(pt_act, 1)
                if not last:
                    take_qk(h + 1, 1 - par)

            for q in range(2):
                act.wait_ge(nat_out[q], 32 * ((NT - q + 1) // 2))
            take_qk(0, 0)
            with act.Fori(0, NH // 2 - 1) as i:
                for par in range(2):
                    act_head(2 * i + par, par, False)
            act_head(NH - 2, 0, False)
            act_head(NH - 1, 1, True)
            for t in range(0, NQ, 2):
                act.wait_ge(ot_done, t + 1)
                nc.scalar.copy(oT[:, :, t * P:(t + 1) * P], psum[:, t % 2, :].rearrange("p (c n) -> p c n", n=P)).then_inc(ot_act, 1)
            for q in range(2):
                act.wait_ge(gate_out[q], 16 * NH)
            with act.Fori(0, NS // 2) as i:
                for par in range(2):
                    b = 2 * i + par
                    for g in range(8):
                        act.wait_ge(kt_done, 8 * b + g + 1)
                        nc.scalar.copy(kt_s[g % 2][:, 0:4, :], psum[:, 0, :].rearrange("p (r n) -> p r n", n=P))
                        nc.scalar.copy(kt_s[g % 2][:, 8, :], psum[:, 5, 0:P]).then_inc(kt_act, 1)
                    act.wait_ge(sx_dve, b + 1)
                    nc.scalar.activation(s_prob, s_prob, ACT.Exp, scale=SCALE).then_inc(sp_act, 1)
                    if par == 0:
                        act.wait_ge(cfill_done, 3 * i + 1)
                        nc.scalar.copy(third(c_sb), fill_ps()).then_inc(c_act, 1)
            act.wait_ge(ue_done, 1)
            nc.scalar.copy(uend_nat[0:10, :], psum[0:10, 1, :]).then_inc(ue_ev, 1)
            with act.Fori(0, KD // 2) as i:
                for par in range(2):
                    for g in range(2):
                        act.wait_ge(gate_ld[2 * par + g], GATE_BASE[2 * par + g] + 16 * i + 16)
                        nc.scalar.activation(gate_in[:, 2 * par + g, :], gate_in[:, 2 * par + g, :], ACT.Sigmoid).then_inc(sg_act, 1)
            for t in range(NT):
                r = rows_of(t)
                act.wait_ge(var_dve, t + 1)
                nc.scalar.activation(rsm[0:r, t % 2, 1:2], rsm[0:r, t % 2, 0:1], ACT.Sqrt).then_inc(sd_act, 1)
                act.wait_ge(ht_done, t + 1)
                if t >= 2:
                    act.wait_ge(lg_done, t - 1)
                for n in range(2):
                    ins = nc.scalar.copy(hT[:, t % 2, 4 * n:4 * n + 4, 0:r], psum[:, 4 + n, :].rearrange("p (k n) -> p k n", n=P)[:, :, 0:r])
                ins.then_inc(ht_act, 1)
            act.wait_ge(sel_dve, NT)
            nc.scalar.activation(gx, gx, ACT.Exp).then_inc(gx_act, 1)

            def rows_turned(par, banks):
                for n in banks:
                    ins = nc.scalar.copy(xgT[:, par, 4 * n:4 * n + 4, :].rearrange("p k n -> p (k n)"), psum[:, n, :])
                return ins

            def gate_sig():
                return nc.scalar.activation(sig, psum[:, 2, :], ACT.Sigmoid)

            def hidden_turned(par):
                return nc.scalar.copy(hhT[:, par, :, :].rearrange("p k n -> p (k n)"), psum[:, 4, :])

            def slots_out(blk, par, out):
                act.dma_start(y_slots[ds(blk * P, P), :], yo[:, par, :]).then_inc(out, 16)

            def down_out(e, half, par, reuse=True):
                act.wait_ge(d_done, e + 1)
                if reuse:
                    act.wait_ge(y_out[par], 16 * half)
                nc.scalar.copy(yo[:, par, 0:512], psum[:, 5, :]).then_inc(y_act, 1)

            def store(e, par):
                act.wait_ge(y_act, e + 1)
                act.wait_ge(y_dve, e + 1)
                slots_out(e, par, y_out[par])

            def act_expert(e, half, par, first=False, last=False, reuse=True):
                act.wait_ge(g_done, e + 1)
                act.wait_ge(gm_dve, e)
                gate_sig().then_inc(gs_act, 1)
                if not last:
                    act.wait_ge(te_done, e + 2)
                    rows_turned(1 - par, (0,)).then_inc(te_act, 1)
                if not first:
                    down_out(e - 1, half + par - 1, 1 - par, reuse)
                act.wait_ge(th_done, e + 1)
                hidden_turned(par).then_inc(th_act, 1)
                if not first:
                    store(e - 1, 1 - par)

            act.wait_ge(te_done, 1)
            rows_turned(0, (0,)).then_inc(te_act, 1)
            act_expert(0, 0, 0, first=True)
            with act.Fori(0, NE // 2 - 1) as i:
                act_expert(2 * i + 1, i, 1)
                act_expert(2 * i + 2, i + 1, 0)
            act_expert(NE - 1, NE // 2 - 1, 1, last=True)
            down_out(NE - 1, NE // 2 - 1, 1)
            store(NE - 1, 1)
            for q in range(2):
                act.wait_ge(y_out[q], 16 * (NE // 2))
            with act.If(act.value_load(ov_on[0:1, 0:1].bitcast(I32), min_val=0, max_val=1)):
                with act.Fori(0, NOVER) as o:
                    on = act.value_load(ov_on[0:1, ds(o, 1)].bitcast(I32), min_val=0, max_val=1)
                    with act.If(on):
                        act.wait_ge(te_done, NE + o + 1)
                        rows_turned(0, (0, 1)).then_inc(te_act, 1)
                        act.wait_ge(g_done, NE + o + 1)
                        gate_sig().then_inc(gs_act, 1)
                        act.wait_ge(th_done, NE + o + 1)
                        hidden_turned(0).then_inc(th_act, 1)
                        act.wait_ge(d_done, NE + o + 1)
                        act.wait_ge(ov_out, 16 * o)
                        nc.scalar.copy(yo[:, 0, 0:512], psum[:, 5, :])
                        nc.scalar.copy(yo[:, 0, 512:D], psum[:, 6, :]).then_inc(y_act, 1)
                        act.wait_ge(y_act, NE + o + 1)
                        slots_out(NE + o, 0, ov_out)
            act.wait_ge(wt_rdy, 1)

            def weighted(t):
                r, s = rows_of(t), t % 3
                act.wait_ge(yg_ld[t % 3], YG_BASE[t % 3] + 32 * (t // 3) + 32)
                nc.scalar.activation(y1[0:r, s, :], y1[0:r, s, :], ACT.Copy, scale=wts[0:r, 0, t:t + 1]).then_inc(y1_act, 1)

            weighted(0)
            weighted(1)
            for t in range(NT):
                r = rows_of(t)
                v = fin[0:r, t % 4, :]
                act.wait_ge(var_dve, NT + t + 1)
                nc.scalar.activation(rsm[0:r, t % 2, 1:2], rsm[0:r, t % 2, 0:1], ACT.Sqrt).then_inc(sd_act, 1)
                if t + 2 < NT:
                    weighted(t + 2)
                act.wait_ge(nb_dve, t + 1)
                nc.scalar.activation(v, v, ACT.Identity, bias=rsm[0:r, t % 2, 3:4], scale=rsm[0:r, t % 2, 2:3]).then_inc(n_act, 1)

        @block.vector
        def _(dve):
            chain = Chain(dve, dve_chain)
            link = chain.link
            tt, stt = nc.vector.tensor_tensor, nc.vector.scalar_tensor_tensor
            for t in range(NT):
                r = rows_of(t)
                dve.wait_ge(xt_done, 2 * t + 2)
                nc.vector.tensor_copy(xT[:, 4:8, t * P:t * P + r],
                                      psum[:, 2 * (t % 2) + 1, :].rearrange("p (k n) -> p k n", n=P)[:, :, 0:r]).then_inc(xt_dve, 1)
            dve.wait_ge(setev[0], 1)
            tt(sq[:, 0, :], ckvT[:, 0, :], ckvT[:, 0, :], ALU.mult).then_inc(sq_ready, 1)
            dve.wait_ge(setev[1], 1)
            tt(sq[:, 1, :], ckvT[:, 1, :], ckvT[:, 1, :], ALU.mult).then_inc(sq_ready, 1)
            dve.wait_ge(consts_in, 16 * N_CONST)
            dve.wait_ge(proj_done, 3)
            link(tt(third(kr_tmp[0:ROPE, 0, :]), bset(0, ROPE), third(cosT[0:ROPE, :]), ALU.mult))
            tt(third(kr_tmp[0:ROPE, 1, :]), bset(0, ROPE, ROPE), third(sinT[ROPE:2 * ROPE, :]), ALU.mult).then_inc(setev[0], 1)
            dve.wait_ge(setev[0], 2)
            link(tt(krT[0:ROPE, :], kr_tmp[0:ROPE, 0, :], kr_tmp[0:ROPE, 1, :], ALU.add))
            for k, (xs, g, n, width, at_step) in enumerate(((ckvT, kvg, 2, CL, SUM_KV), (cqT, qg, 3, QL_, SUM_Q))):
                if k == 1:
                    dve.wait_ge(st_done, 1)
                    nc.vector.tensor_copy(stT, psum[:, 6, 0:64].rearrange("p (j w) -> p j w", w=16)).then_inc(st_ready, 1)
                    dve.wait_ge(st_ready, 1)
                    dve.wait_ge(idx_i, 16)
                    dve.wait_ge(pool_sel, 4)
                    link(nc.vector.tensor_scalar(row_i.bitcast(I32), row_i.bitcast(I32), P // RT - 1, None, ALU.bitwise_and))
                    link(nc.vector.tensor_copy(row_f, row_i.bitcast(I32)))
                    nc.vector.tensor_copy(pt_f, pt_i.bitcast(I32)).then_inc(idx_f, 1)
                    for c in range(3):
                        if c == 2:
                            dve.wait_ge(idx_done, 1)
                            nc.vector.tensor_scalar(cache_idx.bitcast(I32), psum[:, 7, 0:NS * NLD], float(P // RT), row_f, ALU.mult, ALU.add).then_inc(idx_ready, 1)
                        dve.wait_ge(setev[c % 2], (4 + c) // 2 + 1)
                        tt(sq[:, 2 + c, :], cqT[:, c, :], cqT[:, c, :], ALU.mult).then_inc(sq_ready, 1)
                dve.wait_ge(proj_done, at_step + 1)
                nc.vector.tensor_scalar(third(rs[:, k, :]), bset(1), 1.0 / width, RMS_EPS, ALU.mult, ALU.add).then_inc(setev[1], 1)
                dve.wait_ge(std_ready, k + 1)
                link(nc.vector.reciprocal(rs[:, k, :], rs[:, k, :]))
                for c in range(n):
                    ins = stt(out=xs[:, c, :], in0=xs[:, c, :], scalar=g[:, c:c + 1], in1=rs[:, k, :], op0=ALU.mult, op1=ALU.mult)
                    if c < n - 1:
                        link(ins)
                ins.then_inc(norm_ready, 1)
            for par in range(2):
                link(nc.vector.tensor_copy(kT[NOPE:QK, par, :], krT[0:ROPE, 0:SEQ]))

            def rotate(h, par, pair):
                q = qT[:, par, :]
                dve.wait_ge(fill_act, 3 * h + 1)
                link(tt(rope_tmp[NOPE:QK, :], q[QK:P, :], sinT[QK:P, :], ALU.mult))
                link(tt(q[NOPE:QK, :], q[NOPE:QK, :], cosT[NOPE:QK, :], ALU.mult))
                tt(q[NOPE:QK, :], q[NOPE:QK, :], rope_tmp[NOPE:QK, :], ALU.add).then_inc(q_dve, 1)
                nc.vector.tensor_copy(q_bd[NOPE * par:NOPE * (par + 1), ds(pair, 1), par, :].rearrange("p a b -> p (a b)"), q[0:NOPE, SEQ:T])
                dve.wait_ge(q_dve, h + 1)
                for j in range(4):
                    ins = nc.vector.tensor_copy(q_rot[ROPE * j:ROPE * (j + 1), :, j, ds(h, 1)], q[NOPE:QK, SEQ:T].rearrange("p (b o) -> p b o", o=1))
                ins.then_inc(qs_dve, 1)

            def dve_head(h, par, pair, last):
                def soft(i):
                    dve.wait_ge(s_done, NQ * h + i + 1)
                    L = (i + 1) * P
                    link(tt(scores_ps[:, L - P:L], scores_ps[:, L - P:L], mask, ALU.add))
                    link(nc.vector.tensor_reduce(a_max[:, i:i + 1], scores_ps[:, 0:L], AX_X, ALU.max))
                    nc.vector.tensor_scalar(a_neg[:, i:i + 1], a_max[:, i:i + 1], -SCALE, None, ALU.mult).then_inc(max_dve, 1)

                soft(0)
                for i in range(NQ):
                    if i >= 4:
                        dve.wait_ge(pt_done, NQ * h + i + 1)
                        nc.vector.tensor_copy(probT[:, 4:i + 1, :].rearrange("p k n -> p (k n)"), psum[:, 6, 0:(i - 3) * P]).then_inc(pt_dve, 1)
                    if i + 1 < NQ:
                        soft(i + 1)
                    elif not last:
                        rotate(h + 1, 1 - par, pair + par)
                    dve.wait_ge(pv_done, NQ * h + i + 1)
                    link(nc.vector.reciprocal(a_rec[:, i:i + 1], psum[:, 7, VD:VD + 1]))
                    nc.vector.tensor_scalar(o_nat[:, i, ds(h * VD, VD)], psum[:, 7, 0:VD], a_rec[:, i:i + 1], None, ALU.mult).then_inc(o_dve, 1)

            rotate(0, 0, 0)
            LH = 3 * NQ + 2
            with dve.Fori(0, NH // 2 - 1) as i:
                chain.enter(i, 2 * LH)
                for par in range(2):
                    dve_head(2 * i + par, par, i, False)
                chain.leave(NH // 2 - 1)
            dve_head(NH - 2, 0, NH // 2 - 1, False)
            dve_head(NH - 1, 1, NH // 2 - 1, True)
            for t in range(1, NQ, 2):
                dve.wait_ge(ot_done, t + 1)
                nc.vector.tensor_copy(oT[:, :, t * P:(t + 1) * P], psum[:, t % 2, :].rearrange("p (c n) -> p c n", n=P)).then_inc(ot_dve, 1)
            for q in range(2):
                dve.wait_ge(gate_out[q], 16 * NH)
            dve.wait_ge(wt_done, 1)
            link(nc.vector.tensor_copy(wukT[:, 0:2, :], psum[:, 2, :].rearrange("p (i n) -> p i n", n=CL)))
            nc.vector.tensor_copy(wukT[:, 2:4, :], psum[:, 3, :].rearrange("p (i n) -> p i n", n=CL)).then_inc(wt_dve, 1)
            dve.wait_ge(ql_done, 1)
            for c in range(2):
                for hh in range(2):
                    link(nc.vector.tensor_copy(q_lat[:, c, :, hh:NH:2].rearrange("p b i -> p i b"),
                                               psum[:, 4, 0:128].rearrange("p (i c a b) -> p c a i b", i=4, c=2, a=2)[:, c, hh, :, :]))
            for c in range(2):
                link(tt(s_self[:, c, :].rearrange("p (b h) -> p b h", h=NH), q_lat[:, c, :, :],
                        ckvT[:, c, SEQ:T].rearrange("p (b o) -> p b o", o=1).broadcast_to([P, NS, NH]), ALU.mult))
            tt(s_self[0:ROPE, 2, :].rearrange("p (b h) -> p b h", h=NH), q_rot[0:ROPE, :, 0, :],
               krT[0:ROPE, SEQ:T].rearrange("p (b o) -> p b o", o=1).broadcast_to([ROPE, NS, NH]), ALU.mult).then_inc(ss_dve, 1)
            dve.wait_ge(self_done, 1)
            nc.vector.tensor_copy(self_s, psum[:, 4, 256:256 + NS * NH]).then_inc(self_dve, 1)
            link(nc.vector.memset(u_sb[:, 0:2], 0.0))

            def conv_step(j, k):
                g = cw[:, ds(j, 1), k:k + 1].rearrange("p a b -> p (a b)")
                now = u_sb[:, 2 + SEQ:2 + T] if k == 2 else stT[:, ds(j, 1), k:16:2].rearrange("p a b -> p (a b)")
                if k == 0:
                    nc.vector.tensor_scalar(acc[:, 0:SEQ], u_sb[:, 0:SEQ], g, None, ALU.mult)
                    link(nc.vector.tensor_scalar(acc[:, SEQ:T], now, g, None, ALU.mult))
                else:
                    stt(out=acc[:, 0:SEQ], in0=u_sb[:, k:k + SEQ], scalar=g, in1=acc[:, 0:SEQ], op0=ALU.mult, op1=ALU.add)
                    link(stt(out=acc[:, SEQ:T], in0=now, scalar=g, in1=acc[:, SEQ:T], op0=ALU.mult, op1=ALU.add))

            def dve_sample(i, par):
                b = 2 * i + par
                for g in range(8):
                    dve.wait_ge(kt_done, 8 * b + g + 1)
                    nc.vector.tensor_copy(kt_s[g % 2][:, 4:8, :], psum[:, 1, :].rearrange("p (r n) -> p r n", n=P)).then_inc(kt_dve, 1)
                if par == 1:
                    dve.wait_ge(c_act, i + 1)
                    dve.wait_ge(cfill_done, 3 * i + 2)
                    tt(third(u_sb[:, 2:2 + T]), third(c_sb), fill_ps(), ALU.mult).then_inc(cu_dve, 1)
                dve.wait_ge(sc_done, b + 1)
                s_raw = psum[:, 6, 0:NPG * NH].rearrange("p (n h) -> p n h", h=NH)
                wide = lambda v: v.rearrange("p (o h) -> p o h", o=1).broadcast_to([P, NPG, NH])
                nc.vector.tensor_reduce(s_max, s_raw.rearrange("p n h -> p h n"), AX_X, ALU.max).then_inc(smax_dve, 1)
                dve.wait_ge(smax_pool, b + 1)
                own = self_s[:, ds(b * NH, NH)]
                link(tt(s_top, s_all, own, ALU.max))
                tt(s_prob[:, NPG * NH:], own, s_top, ALU.subtract)
                tt(s_prob[:, 0:NPG * NH].rearrange("p (n h) -> p n h", h=NH), s_raw, wide(s_top), ALU.subtract).then_inc(sx_dve, 1)
                dve.wait_ge(sp_act, b + 1)
                nc.vector.tensor_reduce(s_sum, s_prob[:, 0:NPG * NH].rearrange("p (n h) -> p h n", h=NH), AX_X, ALU.add).then_inc(ssum_dve, 1)
                if par == 1:
                    dve.wait_ge(cu_dve, 2 * i + 1)
                    for k in range(3):
                        conv_step(i, k)
                    nc.vector.tensor_copy(uend[:, ds(i, 1), :].rearrange("p a b -> p (a b)"), u_sb[:, SEQ:SEQ + 10])
                    dve.wait_ge(cfill_done, 3 * i + 3)
                    tt(convT[:, ds(i, 1), :].rearrange("p a (b n) -> p (a b) n", n=SP3), third(acc), fill_ps(), ALU.mult).then_inc(cu_dve, 1)
                dve.wait_ge(spv_done, b + 1)
                p_own = s_prob[:, NPG * NH:]
                link(tt(s_tot, p_own, psum[:, 7, 2 * NH:3 * NH], ALU.add))
                link(nc.vector.reciprocal(s_rec, s_tot))
                for c in range(2):
                    link(stt(out=s_o, in0=p_own, scalar=ckvT[:, c, ds(SEQ + b, 1)], in1=psum[:, 7, c * NH:(c + 1) * NH], op0=ALU.mult, op1=ALU.add))
                    ins = tt(o_lat[:, c, ds(b, 1), :].rearrange("p a h -> p (a h)"), s_o, s_rec, ALU.mult)
                    if c == 0:
                        link(ins)
                ins.then_inc(ol_dve, 1)

            with dve.Fori(0, NS // 2) as i:
                chain.enter(i, 2 * 6 + 3)
                for par in range(2):
                    dve_sample(i, par)
                chain.leave(NS // 2)
            dve.wait_ge(os_done, 1)
            for hh in range(2):
                ins = nc.vector.tensor_copy(oT[VD * hh:VD * (hh + 1), :, SEQ:T], psum[0:VD, 0, 0:NH * NS].rearrange("p (i a b) -> p a i b", a=2, b=NS)[:, hh, :, :])
            ins.then_inc(os_dve, 1)
            with dve.Fori(0, KD // 2) as i:
                chain.enter(i, 0)
                for par in range(2):
                    j = 2 * i + par
                    dve.wait_ge(sg_act, 2 * j + 1)
                    dve.wait_ge(y_done, 2 * j + 1)
                    tt(third(gate_in[:, 2 * par, :]), third(gate_in[:, 2 * par, :]), bset(0), ALU.mult).then_inc(yc_dve, 1)
                    dve.wait_ge(sg_act, 2 * j + 2)
                    dve.wait_ge(y_done, 2 * j + 2)
                    tt(third(gate_in[:, 2 * par + 1, :]), third(gate_in[:, 2 * par + 1, :]), bset(1), ALU.mult).then_inc(ya_dve, 1)
                    dve.wait_ge(ya_dve, j + 1)
                    dve.wait_ge(yc_dve, j + 1)
                    tt(mT[:, ds(j, 1), :].rearrange("p a n -> p (a n)"), gate_in[:, 2 * par, :], gate_in[:, 2 * par + 1, :], ALU.add).then_inc(m_dve, 1)
                chain.leave(KD // 2)
            dve.wait_ge(pool_rt, 8)
            link(nc.vector.tensor_copy(iota_f, iota_i.bitcast(I32)))
            link(nc.vector.tensor_copy(tok_f, tok_i.bitcast(I32)))
            link(nc.vector.tensor_scalar(iota_i[:, 0:NE].bitcast(I32), iota_i[:, 0:NE].bitcast(I32), 3, None, ALU.logical_shift_right))
            link(nc.vector.tensor_copy(egroup, iota_i[:, 0:NE].bitcast(I32)))
            ts = nc.vector.tensor_scalar

            def stats(v, r, s):
                link(nc.vector.bn_stats(bst[0:r, 0, :], v[:, 0:512]))
                link(nc.vector.bn_stats(bst[0:r, 1, :], v[:, 512:D]))
                link(nc.vector.bn_aggr(mv[0:r, s, :], bst[0:r]))
                return ts(rsm[0:r, s, 0:1], mv[0:r, s, 1:2], LN_EPS, None, ALU.add)

            def norm1(t):
                r, s = rows_of(t), t % 2
                v = ln_t[0:r, s, :]
                dve.wait_ge(x_ld[t % 3], 16 * (NT // 3 + t // 3 + 1))
                dve.wait_ge(wo_done, t + 1)
                stt(out=v, in0=xr[0:r, t % 3, :], scalar=ALPHA, in1=psum[0:r, 2 * s:2 * s + 2, :].rearrange("p b n -> p (b n)"), op0=ALU.mult, op1=ALU.add).then_inc(r_dve, 1)
                dve.wait_ge(r_dve, t + 1)
                stats(v, r, s).then_inc(var_dve, 1)
                dve.wait_ge(sd_act, t + 1)
                link(nc.vector.reciprocal(rsm[0:r, s, 2:3], rsm[0:r, s, 1:2]))
                link(ts(v, v, mv[0:r, s, 0:1], rsm[0:r, s, 2:3], ALU.subtract, ALU.mult))
                link(tt(v, v, ln1g[0:r], ALU.mult))
                tt(h_sb[0:r, t, :], v, ln1b[0:r], ALU.add).then_inc(h_dve, 1)

            def choose(t):
                r = rows_of(t)
                dve.wait_ge(lg_done, t + 1)
                lgt, let = psum[0:r, 6 + t % 2, 0:NG], psum[0:r, 6 + t % 2, NG:NG + NE]
                tt(lg[0:r, 0:NG], lgt, r_bias[0:r, 0:NG], ALU.add)
                tt(le[0:r], let, r_bias[0:r, NG:NG + NE], ALU.add).then_inc(lg_dve, 1)
                dve.wait_ge(lg_dve, t + 1)
                link(nc.vector.max(g8[0:r], lg[0:r]))
                link(nc.vector.max_index(g8i[0:r].bitcast(U32), g8[0:r], lg[0:r]))
                link(ts(gx[0:r, t, 0:NG], lg[0:r, 0:NG], g8[0:r, 0:1], None, ALU.subtract))
                link(nc.vector.tensor_copy(chosen[0:r, 0:1], g8i[0:r, 0:1].bitcast(U32)))
                link(ts(lem[0:r], egroup[0:r], chosen[0:r, 0:1], -3e38, ALU.not_equal, ALU.mult))
                link(tt(lem[0:r], lem[0:r], le[0:r], ALU.add))
                link(nc.vector.max(t8[0:r], lem[0:r]))
                link(nc.vector.max_index(t8i[0:r].bitcast(U32), t8[0:r], lem[0:r]))
                link(tt(gx[0:r, t, NG:NG + 1], t8[0:r, 1:2], t8[0:r, 0:1], ALU.subtract))
                link(nc.vector.tensor_copy(chosen[0:r, 1:3], t8i[0:r, 0:2].bitcast(U32)))
                for k, m in enumerate((m1, m2)):
                    link(ts(m[0:r, t, :], iota_f[0:r, 0:NE], chosen[0:r, 1 + k:2 + k], None, ALU.is_equal))
                link(tt(m12[0:r, t, :], m1[0:r, t, :], m2[0:r, t, :], ALU.add))
                tt(cum[:, t + 1, :], cum[:, t, :], m12[:, t, :], ALU.add).then_inc(sel_dve, 1)
                dve.wait_ge(sel_dve, t + 1)

            dve.wait_ge(ln1_ld, 96)
            norm1(0)
            for t in range(1, NT):
                norm1(t)
                choose(t - 1)
            choose(NT - 1)
            dve.wait_ge(pos_done, 1)
            link(nc.vector.tensor_copy(r_pos.rearrange("p t e -> p (t e)"), psum[:, 0, 0:NT * NE]))
            link(nc.vector.memset(extra, 0.0))
            for j in range(1, -(-T // P)):
                link(stt(out=extra, in0=psum[:, 1, 0:NE], scalar=float(P * j), in1=extra, op0=ALU.is_gt, op1=ALU.add))
            link(nc.vector.tensor_copy(ob[:, 0, :], extra))
            step, cur = 1, 0
            while step < NE:
                link(nc.vector.tensor_copy(ob[:, 1 - cur, 0:step], ob[:, cur, 0:step]))
                link(tt(ob[:, 1 - cur, step:NE], ob[:, cur, step:NE], ob[:, cur, 0:NE - step], ALU.add))
                step, cur = 2 * step, 1 - cur
            total = ob[:, cur, :]
            link(tt(skip, total, extra, ALU.subtract))
            link(tt(skip, skip, iota_f[:, 0:NE], ALU.subtract))
            link(ts(skip, skip, float(NE - 1), float(P), ALU.add, ALU.mult))
            over_t = lambda v: v.rearrange("p (o e) -> p o e", o=1).broadcast_to([P, NT, NE])
            link(ts(r_t, r_pos, float(P), None, ALU.is_ge))
            link(tt(r_t, r_t, over_t(skip), ALU.mult))
            link(stt(out=r_d, in0=over_t(iota_f[:, 0:NE]), scalar=float(P), in1=r_pos, op0=ALU.mult, op1=ALU.add))
            link(tt(r_d, r_d, r_t, ALU.add))
            for k, m in enumerate((m1, m2)):
                link(tt(r_t, r_d, m, ALU.mult))
                link(nc.vector.tensor_reduce(d_f[:, k, :], r_t, AX_X, ALU.add))
            link(nc.vector.tensor_copy(slot_of.bitcast(I32), d_f))
            link(ts(row_i2.bitcast(I32), slot_of.bitcast(I32), P - 1, None, ALU.bitwise_and))
            link(ts(blk_i.bitcast(I32), slot_of.bitcast(I32), 7, None, ALU.logical_shift_right))
            link(nc.vector.tensor_copy(row_f2, row_i2.bitcast(I32)))
            link(nc.vector.tensor_copy(blk_f, blk_i.bitcast(I32)))
            wide = lambda v, c: v.rearrange("p k (t o) -> p (k t) o", o=1).broadcast_to([P, 2 * NT, c])
            link(tt(oh_blk, iota_f[:, 0:NBLK].rearrange("p (o c) -> p o c", o=1).broadcast_to([P, 2 * NT, NBLK]), wide(blk_f, NBLK), ALU.is_equal))
            for k in range(2):
                link(tt(oh_blk[:, k * NT:(k + 1) * NT, :], oh_blk[:, k * NT:(k + 1) * NT, :],
                        tok_f.rearrange("p (t o) -> p t o", o=1).broadcast_to([P, NT, NBLK]), ALU.mult))
            for n in range(0, 2 * NT, OH):
                tt(oh_row[:, n:n + OH, :], iota_f.rearrange("p (o c) -> p o c", o=1).broadcast_to([P, OH, P]),
                   wide(row_f2, P)[:, n:n + OH, :], ALU.is_equal).then_inc(oh_dve, 1)
            over_o = lambda v: v.rearrange("p (o e) -> p o e", o=1).broadcast_to([P, NOVER, NE])
            link(tt(o_cmp, over_o(total), iota_f[:, 0:NOVER].rearrange("p (o e) -> p o e", e=1).broadcast_to([P, NOVER, NE]), ALU.is_le))
            link(nc.vector.tensor_reduce(ov_f, o_cmp, AX_X, ALU.add))
            link(ts(ov_e.bitcast(I32), ov_f, float(NE - 1), None, ALU.min))
            link(ts(ov_on.bitcast(I32), iota_f[:, 0:NOVER], total[:, NE - 1:NE], None, ALU.is_lt))
            dve.wait_ge(tb_done, 1)
            nc.vector.tensor_copy(blk_tok.bitcast(I32), psum[:, 2, 0:NBLK]).then_inc(blk_dve, 1)
            dve.wait_ge(gx_act, 1)
            e2 = gx[:, :, NG:NG + 1].rearrange("p t o -> p (t o)")
            link(nc.vector.tensor_reduce(p_sum, gx[:, :, 0:NG], AX_X, ALU.add))
            link(ts(wts[:, 0, :], e2, 1.0, None, ALU.add))
            link(tt(wts[:, 0, :], wts[:, 0, :], p_sum, ALU.mult))
            link(nc.vector.reciprocal(wts[:, 0, :], wts[:, 0, :]))
            tt(wts[:, 1, :], wts[:, 0, :], e2, ALU.mult).then_inc(wt_rdy, 1)
            dve.wait_ge(wt_rdy, 1)

            def swiglu(e, par):
                dve.wait_ge(gs_act, e + 1)
                tt(act_t, sig, psum[:, 2, :], ALU.mult).then_inc(gm_dve, 1)
                dve.wait_ge(gm_dve, e + 1)
                dve.wait_ge(u_done, e + 1)
                tt(hid[:, par, :], act_t, psum[:, 3, :], ALU.mult).then_inc(hu_dve, 1)

            def rows_right(e, par):
                dve.wait_ge(te_done, e + 1)
                nc.vector.tensor_copy(xgT[:, par, 4:8, :].rearrange("p k n -> p (k n)"), psum[:, 1, :]).then_inc(te_dve, 1)

            def down_right(e, half, par):
                dve.wait_ge(d_done, e + 1)
                dve.wait_ge(y_out[par], 16 * half)
                nc.vector.tensor_copy(yo[:, par, 512:D], psum[:, 6, :]).then_inc(y_dve, 1)

            rows_right(0, 0)
            swiglu(0, 0)
            rows_right(1, 1)
            with dve.Fori(0, NE // 2 - 1) as i:
                for par in (1, 0):
                    e, half = (2 * i + 1, i) if par else (2 * i + 2, i + 1)
                    dve.wait_ge(th_done, e - 1)
                    swiglu(e, par)
                    rows_right(e + 1, 1 - par)
                    down_right(e - 1, half + par - 1, 1 - par)
            dve.wait_ge(th_done, NE - 2)
            swiglu(NE - 1, 1)
            down_right(NE - 2, NE // 2 - 1, 0)
            down_right(NE - 1, NE // 2 - 1, 1)
            dve.wait_ge(th_done, NE)
            with dve.If(dve.value_load(ov_on[0:1, 0:1].bitcast(I32), min_val=0, max_val=1)):
                with dve.Fori(0, NOVER) as o:
                    on = dve.value_load(ov_on[0:1, ds(o, 1)].bitcast(I32), min_val=0, max_val=1)
                    with dve.If(on):
                        dve.wait_ge(gs_act, NE + o + 1)
                        tt(act_t, sig, psum[:, 2, :], ALU.mult).then_inc(gm_dve, 1)
                        dve.wait_ge(gm_dve, NE + o + 1)
                        dve.wait_ge(u_done, NE + o + 1)
                        tt(hid[:, 0, :], act_t, psum[:, 3, :], ALU.mult).then_inc(hu_dve, 1)
            dve.wait_ge(ln1_ld, 96 + 32)

            def summed(t):
                r, s = rows_of(t), t % 2
                v = fin[0:r, t % 4, :]
                if t >= 4:
                    dve.wait_ge(f_out[t % 4], F_BASE[t % 4] + 16 * (t // 4))
                dve.wait_ge(yg_ld[t % 3], YG_BASE[t % 3] + 32 * (t // 3) + 32)
                dve.wait_ge(y1_act, t + 1)
                stt(out=v, in0=y2[0:r, t % 3, :], scalar=wts[0:r, 1, t:t + 1], in1=y1[0:r, t % 3, :], op0=ALU.mult, op1=ALU.add).then_inc(sum_dve, 1)
                dve.wait_ge(sum_dve, t + 1)
                link(stt(out=v, in0=h_sb[0:r, t, :], scalar=ALPHA, in1=v, op0=ALU.mult, op1=ALU.add))
                stats(v, r, s).then_inc(var_dve, 1)

            def factors(t):
                r, s = rows_of(t), t % 2
                dve.wait_ge(sd_act, NT + t + 1)
                link(nc.vector.reciprocal(rsm[0:r, s, 2:3], rsm[0:r, s, 1:2]))
                stt(out=rsm[0:r, s, 3:4], in0=mv[0:r, s, 0:1], scalar=-1.0, in1=rsm[0:r, s, 2:3], op0=ALU.mult, op1=ALU.mult).then_inc(nb_dve, 1)

            def scaled(t):
                r = rows_of(t)
                v = fin[0:r, t % 4, :]
                dve.wait_ge(n_act, t + 1)
                tt(v, v, ln2g[0:r], ALU.mult).then_inc(g_dve, 1)

            summed(0)
            for t in range(NT):
                if t + 1 < NT:
                    summed(t + 1)
                factors(t)
                if t >= 1:
                    scaled(t - 1)
            scaled(NT - 1)


INS = ["x_prompt", "x_sample", "cache_ckv", "cache_krope", "state_conv", "page_table", "w_in", "conv_w", "q_norm_g",
       "w_uq", "kv_norm_g", "w_uk", "w_uv", "w_br_conv", "w_br_attn", "w_o", "ln1_g", "ln1_b", "router_w_group",
       "router_b_group", "router_w_expert", "router_b_expert", "w_gate", "w_up", "w_down", "ln2_g", "ln2_b"]
OUTS = [("y_prompt", (1, SEQ, D)), ("y_sample", (NS, 1, D)), ("new_ckv_prompt", (1, 1, SEQ, CL)),
        ("new_krope_prompt", (1, 1, SEQ, ROPE)), ("new_conv_prompt", (1, 1, 2, DC)),
        ("new_ckv_sample", (1, NS, 1, CL)), ("new_krope_sample", (1, NS, 1, ROPE)), ("new_conv_sample", (1, NS, 2, DC))]


def rope_tables():
    pos = np.concatenate([np.arange(SEQ), np.full(NS, PAST)]).astype(np.float32)
    half = ROPE // 2
    inv = (np.float32(10000.0) ** (-(np.arange(half, dtype=np.float32) * np.float32(2.0) / np.float32(ROPE)))).astype(np.float32)
    ang = inv[np.arange(P) % half][:, None] * pos[None, :]
    sign = np.where(np.arange(P) % ROPE < half, -1.0, 1.0).astype(np.float32)[:, None]
    return np.cos(ang).astype(np.float32), (sign * np.sin(ang)).astype(np.float32)


def kernel(**inputs):
    import concourse.bacc as bacc
    from concourse.bass_utils import run_bass_kernel_spmd

    nc = bacc.Bacc("TRN2", target_bir_lowering=False, num_devices=1)
    arrays = {n: np.ascontiguousarray(inputs[n]) for n in INS}
    arrays["cos_table"], arrays["sin_table"] = rope_tables()
    a = {}
    for n, v in arrays.items():
        a[n] = nc.dram_tensor(f"in_{n}", v.shape, mybir.dt.from_np(v.dtype), kind="ExternalInput").ap()
    for i, (n, shape) in enumerate(OUTS):
        a[n] = nc.dram_tensor(f"out_{i}_dram", shape, F32, kind="ExternalOutput").ap()
    build(nc, a)
    r = run_bass_kernel_spmd(nc, [{f"in_{n}": v for n, v in arrays.items()}], core_ids=[0])
    return tuple(r.results[0][f"out_{i}_dram"] for i in range(len(OUTS)))
```
